# Optimizing a Trainium2 kernel written in Bass

```python
import jax, jax.numpy as jnp
from jax import lax
import numpy as np

D_MODEL = 2048
BATCH = 1
SEQ = 256
DEPTH = 1

CHUNK = 64
Q_BLOCK = 128
EPS = 1e-6

MLA_HEADS = 8
MLA_NOPE = 128
MLA_ROPE = 64
MLA_V = 128
MLA_Q_LORA = 512
MLA_KV_LORA = 512
ROPE_THETA = 10000.0
MLA_WIDTH = MLA_HEADS * MLA_V

POOL_WINDOWS = (2, 4, 8, 16)
POOL_GROUPS = 4
POOL_GROUP_W = 256
POOL_WIDTH = POOL_GROUPS * POOL_GROUP_W

GLA_HEADS = 4
GLA_DK = 128
GLA_DV = 256
GLA_GATE_RANK = 16
GLA_GATE_TAU = 16.0
GLA_QK_WIDTH = GLA_HEADS * GLA_DK
GLA_WIDTH = GLA_HEADS * GLA_DV

N_BRANCH = 3
BRANCH_WIDTH = 1024

SPLIT_SIZES = (MLA_Q_LORA, MLA_KV_LORA, MLA_ROPE, MLA_WIDTH,
               POOL_WIDTH, POOL_WIDTH,
               GLA_QK_WIDTH, GLA_QK_WIDTH, GLA_WIDTH,
               GLA_GATE_RANK, GLA_WIDTH,
               N_BRANCH * D_MODEL)
N_IN = sum(SPLIT_SIZES)

kernel_name = "hybrid_mla_pool_gla_gated_merge"

def _split_points():
    pts, acc = [], 0
    for s in SPLIT_SIZES[:-1]:
        acc += s
        pts.append(acc)
    return pts

def rmsnorm(x, g):
    xf = x.astype(jnp.float32)
    y = xf * lax.rsqrt(jnp.mean(xf * xf, axis=-1, keepdims=True) + EPS)
    return (y * g.astype(jnp.float32)).astype(x.dtype)

def rope_tables(positions):
    inv = 1.0 / (ROPE_THETA ** (jnp.arange(0, MLA_ROPE, 2, dtype=jnp.float32) / MLA_ROPE))
    ang = positions.astype(jnp.float32)[..., None] * inv
    return jnp.cos(ang)[:, :, None, :], jnp.sin(ang)[:, :, None, :]

def apply_rope(x, cos, sin):
    xf = x.astype(jnp.float32)
    x1, x2 = jnp.split(xf, 2, axis=-1)
    return jnp.concatenate([x1 * cos - x2 * sin, x2 * cos + x1 * sin], axis=-1).astype(x.dtype)

def block_causal_attention(q, k, v):
    B, S, H, Dq = q.shape
    Dv = v.shape[-1]
    nb = S // Q_BLOCK
    scale = Dq ** -0.5
    qb = q.reshape(B, nb, Q_BLOCK, H, Dq).transpose(1, 0, 2, 3, 4)
    k_chunk = jnp.arange(S) // CHUNK

    def one_block(args):
        qi, i = args
        q_chunk = (i * Q_BLOCK + jnp.arange(Q_BLOCK)) // CHUNK
        mask = k_chunk[None, :] <= q_chunk[:, None]
        s = jnp.einsum('bqhd,bkhd->bhqk', qi, k).astype(jnp.float32) * scale
        s = jnp.where(mask[None, None], s, -1e30)
        p = jax.nn.softmax(s, axis=-1).astype(v.dtype)
        return jnp.einsum('bhqk,bkhv->bqhv', p, v)

    out = lax.map(one_block, (qb, jnp.arange(nb)))
    return out.transpose(1, 0, 2, 3, 4).reshape(B, S, H, Dv)

def mla_branch(c_q, c_kv, k_rope_raw, q_norm_g, kv_norm_g, w_uq, w_ukv, cos, sin):
    B, S, _ = c_q.shape
    q = (rmsnorm(c_q, q_norm_g) @ w_uq).reshape(B, S, MLA_HEADS, MLA_NOPE + MLA_ROPE)
    q_nope, q_rope = q[..., :MLA_NOPE], q[..., MLA_NOPE:]
    q = jnp.concatenate([q_nope, apply_rope(q_rope, cos, sin)], axis=-1)
    kv = (rmsnorm(c_kv, kv_norm_g) @ w_ukv).reshape(B, S, MLA_HEADS, MLA_NOPE + MLA_V)
    k_nope, v = kv[..., :MLA_NOPE], kv[..., MLA_NOPE:]
    k_rope = apply_rope(k_rope_raw[:, :, None, :], cos, sin)
    k = jnp.concatenate([k_nope, jnp.broadcast_to(k_rope, (B, S, MLA_HEADS, MLA_ROPE))], axis=-1)
    o = block_causal_attention(q, k, v)
    return o.reshape(B, S, MLA_WIDTH)

def pool_branch(u, pool_w, pool_scale):
    B, S, _ = u.shape
    uf = u.astype(jnp.float32).reshape(B, S, POOL_GROUPS, POOL_GROUP_W)
    cs = jnp.cumsum(uf, axis=1)
    t = jnp.arange(S)
    mixed = []
    for g, w in enumerate(POOL_WINDOWS):
        csg = cs[:, :, g]
        shifted = jnp.pad(csg, ((0, 0), (w, 0), (0, 0)))[:, :S]
        count = jnp.minimum(t + 1, w).astype(jnp.float32)[None, :, None]
        mixed.append((csg - shifted) / count - uf[:, :, g])
    m = jnp.stack(mixed, axis=2).astype(u.dtype)
    y = jnp.einsum('bsgc,gcd->bsgd', m, pool_w).reshape(B, S, POOL_WIDTH)
    return y * pool_scale

def gla_branch(q, k, v, gate_lr, w_gate, b_gate, norm_g):
    B, S, _ = q.shape
    N, L, H = S // CHUNK, CHUNK, GLA_HEADS
    f32 = jnp.float32
    qc = q.astype(f32).reshape(B, N, L, H, GLA_DK) * (GLA_DK ** -0.5)
    kc = k.astype(f32).reshape(B, N, L, H, GLA_DK)
    vc = v.astype(f32).reshape(B, N, L, H, GLA_DV)
    log_a = jax.nn.log_sigmoid((gate_lr @ w_gate + b_gate).astype(f32)) / GLA_GATE_TAU
    log_a = log_a.reshape(B, N, L, H, GLA_DK)
    bcum = jnp.cumsum(log_a, axis=2)
    b_last = bcum[:, :, -1:]
    q_dec = qc * jnp.exp(bcum)
    k_dec = kc * jnp.exp(-bcum)
    tril = jnp.tril(jnp.ones((L, L), dtype=bool))
    att = jnp.einsum('bnihd,bnjhd->bnhij', q_dec, k_dec)
    att = jnp.where(tril[None, None, None], att, 0.0)
    o_intra = jnp.einsum('bnhij,bnjhv->bnihv', att, vc)
    k_end = kc * jnp.exp(b_last - bcum)
    U = jnp.einsum('bnjhd,bnjhv->nbhdv', k_end, vc)
    decay = jnp.exp(b_last[:, :, 0]).transpose(1, 0, 2, 3)

    def step(state, inp):
        d, u_c = inp
        return d[..., None] * state + u_c, state

    _, s_prev = lax.scan(step, jnp.zeros((B, H, GLA_DK, GLA_DV), f32), (decay, U))
    o_inter = jnp.einsum('bnihd,nbhdv->bnihv', q_dec, s_prev)
    o = (o_intra + o_inter).reshape(B, S, H, GLA_DV)
    o = o * lax.rsqrt(jnp.mean(o * o, axis=-1, keepdims=True) + EPS)
    return (o.reshape(B, S, GLA_WIDTH) * norm_g.astype(f32)).astype(q.dtype)

def hybrid_layer(x, cos, sin, norm_g, w_in, b_merge, mla_q_norm, mla_kv_norm, mla_w_uq, mla_w_ukv,
                 pool_w, pool_scale, gla_w_gate, gla_b_gate, gla_norm, w_branch, w_out):
    B, S, D = x.shape
    h = rmsnorm(x, norm_g)
    proj = h @ w_in
    (c_q, c_kv, k_rope, z_a, u_b, z_b, q_c, k_c, v_c, gate_lr, z_c, gates) = jnp.split(proj, _split_points(), axis=-1)
    y_a = mla_branch(c_q, c_kv, k_rope, mla_q_norm, mla_kv_norm, mla_w_uq, mla_w_ukv, cos, sin) * jax.nn.silu(z_a)
    y_b = pool_branch(u_b, pool_w, pool_scale) * jax.nn.silu(z_b)
    y_c = gla_branch(q_c, k_c, v_c, gate_lr, gla_w_gate, gla_b_gate, gla_norm) * jax.nn.silu(z_c)
    ys = jnp.stack([y_a, y_b, y_c], axis=2)
    p = jnp.einsum('bsnw,nwd->bsnd', ys, w_branch)
    g = jax.nn.sigmoid(gates.reshape(B, S, N_BRANCH, D) + b_merge)
    merged = jnp.sum(g * p, axis=2)
    return x + merged @ w_out

def setup_inputs(seed: int = 0) -> dict:
    key = jax.random.key(seed)
    ks = jax.random.split(key, 16)
    f32 = jnp.float32

    def nrm(k, shape, fan_in):
        return jax.random.normal(k, shape, f32) * (fan_in ** -0.5)

    def gain(k, shape):
        return 1.0 + 0.02 * jax.random.normal(k, shape, f32)

    return {
        "x": jax.random.normal(ks[0], (BATCH, SEQ, D_MODEL), f32),
        "positions": jnp.broadcast_to(jnp.arange(SEQ, dtype=jnp.int32)[None, :], (BATCH, SEQ)),
        "norm_g": gain(ks[1], (DEPTH, D_MODEL)),
        "w_in": nrm(ks[2], (DEPTH, D_MODEL, N_IN), D_MODEL),
        "b_merge": 0.02 * jax.random.normal(ks[3], (DEPTH, N_BRANCH, D_MODEL), f32),
        "mla_q_norm": gain(ks[4], (DEPTH, MLA_Q_LORA)),
        "mla_kv_norm": gain(ks[5], (DEPTH, MLA_KV_LORA)),
        "mla_w_uq": nrm(ks[6], (DEPTH, MLA_Q_LORA, MLA_HEADS * (MLA_NOPE + MLA_ROPE)), MLA_Q_LORA),
        "mla_w_ukv": nrm(ks[7], (DEPTH, MLA_KV_LORA, MLA_HEADS * (MLA_NOPE + MLA_V)), MLA_KV_LORA),
        "pool_w": nrm(ks[8], (DEPTH, POOL_GROUPS, POOL_GROUP_W, POOL_GROUP_W), POOL_GROUP_W),
        "pool_scale": gain(ks[9], (DEPTH, POOL_WIDTH)),
        "gla_w_gate": nrm(ks[10], (DEPTH, GLA_GATE_RANK, GLA_QK_WIDTH), GLA_GATE_RANK),
        "gla_b_gate": 0.02 * jax.random.normal(ks[11], (DEPTH, GLA_QK_WIDTH), f32),
        "gla_norm": gain(ks[12], (DEPTH, GLA_WIDTH)),
        "w_branch": nrm(ks[13], (DEPTH, N_BRANCH, BRANCH_WIDTH, D_MODEL), BRANCH_WIDTH),
        "w_out": nrm(ks[14], (DEPTH, D_MODEL, D_MODEL), D_MODEL),
        "final_norm": gain(ks[15], (D_MODEL,)),
    }

def reference(x, positions, norm_g, w_in, b_merge, mla_q_norm, mla_kv_norm, mla_w_uq, mla_w_ukv,
              pool_w, pool_scale, gla_w_gate, gla_b_gate, gla_norm, w_branch, w_out, final_norm):
    cos, sin = rope_tables(positions)
    h = x
    for l in range(DEPTH):
        h = hybrid_layer(h, cos, sin, norm_g[l], w_in[l], b_merge[l], mla_q_norm[l], mla_kv_norm[l],
                         mla_w_uq[l], mla_w_ukv[l], pool_w[l], pool_scale[l], gla_w_gate[l],
                         gla_b_gate[l], gla_norm[l], w_branch[l], w_out[l])
    return rmsnorm(h, final_norm)


_drawn_inputs = setup_inputs


def setup_inputs(seed=0):
    import zlib

    import numpy as np

    out = dict(_drawn_inputs(seed))
    spreads = {}
    factors = {'norm_g': 3.685,
     'b_merge': 8.0,
     'mla_q_norm': 50.145,
     'mla_kv_norm': 48.646,
     'pool_scale': 95.559,
     'gla_b_gate': 41.222,
     'gla_norm': 200.0,
     'final_norm': 20.689}
    for name, (base, spread) in spreads.items():
        noise = np.random.default_rng([zlib.crc32(name.encode()), seed]).standard_normal(out[name].shape)
        drawn = base * np.exp(spread * noise) if base else spread * noise
        out[name] = __import__('jax').numpy.asarray(drawn.astype(out[name].dtype))
    for name, factor in factors.items():
        out[name] = (out[name] * factor).astype(out[name].dtype)
    return out
```

```python
from contextlib import ExitStack

import numpy as np

import concourse.bass as bass
from concourse import mybir
from concourse.alu_op_type import AluOpType as ALU

ACT = mybir.ActivationFunctionType
F32 = mybir.dt.float32
F32R = mybir.dt.float32r
I32 = mybir.dt.int32
AX_X = mybir.AxisListType.X

P = 128
D = 2048
SEQ = 256
TB = SEQ // P
CHUNK = 64
EPS = 1e-6
HEADS, NOPE, ROPE, DV = 8, 128, 64, 128
LORA = 512
G_HEADS, G_DK, G_DV, G_RANK, G_TAU = 4, 128, 256, 16, 16.0
WINDOWS = (2, 4, 8, 16)
WIDTH = 1024
NEG = -1e30

C_Q, C_KV, C_KROPE, C_ZA = 0, LORA, 2 * LORA, 2 * LORA + ROPE
C_UB = C_ZA + WIDTH
C_ZB = C_UB + WIDTH
C_QC = C_ZB + WIDTH
C_KC = C_QC + LORA
C_VC = C_KC + LORA
C_LR = C_VC + WIDTH
C_ZC = C_LR + G_RANK
C_GATES = C_ZC + WIDTH

NCOL = 512
KT = D // P
WKT = WIDTH // P
SLOT = 1024
RING = 4

S_PROJ = 0
N_PAIRS = 6
S_SMALL = S_PROJ + 16 * N_PAIRS
S_ZC = S_SMALL + 4
ZC_SLOTS = ("z", "z", "z", "z", "z", "z", "z", "p", "p", "z", "z", "p", "p", "z", "z", "z", "z", "z", "z", "z")
S_B0 = S_ZC + 20
S_B1 = S_B0 + 64
S_B2 = S_B1 + 48
S_OUT = S_B2 + 48
S_END = S_OUT + 32

A_X = 0
A_KR, A_GT = 8, 9
A_CT = 10
A_LG = 14
A_BAND = 16
A_PW = 20
A_YB = 24
A_QK = 28
A_B0 = 32
A_B1 = A_B0 + 48
A_MT = A_B1 + 32

ZC_TASKS = {1: (8, 9), 2: (10, 11), 3: (12, 13), 4: (14, 15), 5: (16, 17), 6: (18, 19), 7: (20,), 8: (21,),
            11: (22,), 12: (23,), 13: (24, 25), 15: (26, 27), 16: (28, 29), 18: (30, 31)}

M_RNE = 12582912.0
TWO_PI = 2 * np.pi


def _top(x, bits):
    m, e = np.frexp(x)
    return float(np.ldexp(np.round(np.ldexp(m, bits)), int(e) - bits))


PI1 = _top(TWO_PI, 14)
PI2 = _top(TWO_PI - PI1, 14)
PI3 = float(np.float32(TWO_PI - PI1 - PI2))
TURNS = []
for _j in (3, 2, 1):
    _t = 2.0 ** (8 * _j) / TWO_PI
    _t -= np.rint(_t)
    TURNS.append((2.0 ** (8 * _j), _top(_t, 15), float(np.float32(_t - _top(_t, 15)))))

K_ID, K_MASK, K_FREQ, K_SIGN, K_BAND = 0, 128, 384, 385, 386
K_END = K_BAND + 4 * 384


def shape_constants():
    c = np.zeros((P, K_END), np.float32)
    c[:, K_ID:K_ID + P] = np.eye(P, dtype=np.float32)
    c[:CHUNK, K_MASK + 2 * P - CHUNK:K_MASK + 2 * P] = NEG
    half = ROPE // 2
    inv = (np.float32(1.0) / (np.float32(10000.0) ** (np.arange(0, ROPE, 2, dtype=np.float32) / np.float32(ROPE))))
    c[:, K_FREQ] = inv[np.arange(P) % half]
    c[:, K_SIGN] = 1.0
    c[2 * half:3 * half, K_SIGN] = -1.0
    t = np.arange(SEQ)
    for g, w in enumerate(WINDOWS):
        count = np.minimum(t + 1, w).astype(np.float32)
        band = ((t[:, None] <= t[None, :]) & (t[:, None] > t[None, :] - w)) / count[None, :] - np.eye(SEQ)
        c[:, K_BAND + g * 384:K_BAND + g * 384 + 256] = band[:P]
        c[:, K_BAND + g * 384 + 256:K_BAND + g * 384 + 384] = band[P:, P:]
    return c


def trunk_kernel(nc, x, positions, norm_g, w_in, b_merge, mla_q_norm, mla_kv_norm, mla_w_uq, mla_w_ukv, pool_w,
                 pool_scale, gla_w_gate, gla_b_gate, gla_norm, w_branch, w_out, final_norm, consts, out):
    x_d = x[0].rearrange("(b p) d -> p b d", p=P)
    out_d = out[0].rearrange("(b p) d -> p b d", p=P)
    w_in_d = w_in[0].rearrange("(t p) n -> p t n", p=P)
    w_uq_d = mla_w_uq[0].rearrange("(t p) n -> p t n", p=P)
    w_ukv_d = mla_w_ukv[0].rearrange("(t p) (h c n) -> p t h c n", p=P, h=HEADS, c=2)
    pool_w_d = pool_w[0].rearrange("g (t p) n -> g p t n", p=P)
    w_branch_d = [w_branch[0, n].rearrange("(t p) n -> p t n", p=P) for n in range(3)]
    w_out_d = w_out[0].rearrange("(t p) n -> p t n", p=P)

    with ExitStack() as ctx:
        def sb(name, shape, dt=F32):
            return ctx.enter_context(nc.sbuf_tensor(name, shape, dt))

        def sem(name):
            return ctx.enter_context(nc.semaphore(name))

        xT_hi = sb("xT_hi", [P, KT, SEQ], F32R)
        xT_lo = sb("xT_lo", [P, KT, SEQ], F32R)
        y0_hi = sb("y0_hi", [P, WKT, SEQ], F32R)
        y0_lo = sb("y0_lo", [P, WKT, SEQ], F32R)
        y1_hi = sb("y1_hi", [P, WKT, SEQ], F32R)
        y1_lo = sb("y1_lo", [P, WKT, SEQ], F32R)
        cT_hi = sb("cT_hi", [P, 8, SEQ], F32R)
        cT_lo = sb("cT_lo", [P, 8, SEQ], F32R)
        raw = sb("raw", [P, RING, SLOT])
        w_hi = sb("w_hi", [P, RING, SLOT], F32R)
        w_lo = sb("w_lo", [P, RING, SLOT], F32R)
        xin = sb("xin", [P, TB, D])
        proj = sb("proj", [P, TB, 12 * NCOL])
        head_a = sb("head_a", [P, 1792])
        head_pT_b = sb("head_pT_b", [P, 3, P])
        yh = sb("yh", [P, TB, 2 * P])
        const = sb("const", [P, K_BAND])
        rope_tab = sb("rope_tab", [P, SEQ])
        krT = sb("krT", [ROPE, SEQ])
        kr_tok = sb("kr_tok", [P, TB, 144])
        gains = sb("gains", [P, 44])
        stat = sb("stat", [P, 64])

        ident = const[:, K_ID:K_ID + P]
        mask = const[:, K_MASK:K_MASK + SEQ]
        g_norm, g_q, g_kv, g_pool, g_gla, b_gate = (gains[:, a:b] for a, b in
                                                    ((0, 16), (16, 20), (20, 24), (24, 32), (32, 40), (40, 44)))
        ssq_x, rstd_x, ssq_c, rstd_c = stat[:, 0:2], stat[:, 2:4], stat[:, 4:8], stat[:, 8:12]
        minus_half = stat[:, 12:16]
        mx = [stat[:, 16:18], stat[:, 18:20]]
        neg_m = [stat[:, 20:22], stat[:, 22:24]]
        row_sum = [stat[:, 24:26], stat[:, 26:28]]
        row_inv = [stat[:, 28:30], stat[:, 30:32]]
        b_last, decay, ssq_o, rstd_o = stat[:, 32:36], stat[:, 36:40], stat[:, 40:42], stat[:, 42:44]
        ssq_f, ssq_ft, rstd_f = stat[:, 44:52], stat[:, 52:54], stat[:, 54:56]
        ms_tmp = stat[:, 56:60]

        R_C, R_ZA, R_U, R_ZB, R_QK, R_V = (n * WIDTH for n in range(6))
        c_tok = proj[:, :, R_C:R_C + WIDTH]
        zc = c_tok
        za = proj[:, :, R_ZA:R_ZA + WIDTH]
        u_tok = proj[:, :, R_U:R_U + WIDTH]
        zb = proj[:, :, R_ZB:R_ZB + WIDTH]
        v_tok = proj[:, :, R_V:R_V + WIDTH]
        qT_all = proj[:, 0, R_U:R_U + WIDTH].rearrange("p (h t) -> p h t", h=G_HEADS)
        kT_all = proj[:, 1, R_U:R_U + WIDTH].rearrange("p (h t) -> p h t", h=G_HEADS)
        bcum = proj[:, 0, R_ZB:R_ZB + WIDTH].rearrange("p (h t) -> p h t", h=G_HEADS)
        head_b = proj[:, 1, R_ZB:R_ZB + WIDTH]
        gate = proj[:, 0, R_QK:R_QK + WIDTH].rearrange("p (b n) -> p b n", b=TB)
        bias_row = proj[:, 1, R_QK:R_QK + NCOL]
        s_b = proj[:, 1, R_QK + NCOL:R_QK + NCOL + 384]
        x_res = proj[:, :, 0:D]
        fnorm_row = proj[:, 0, R_U:R_U + D]
        band = xin[:, 0, 0:4 * 384].rearrange("p (g t) -> p g t", g=4)
        w_gate = xin[0:G_RANK, 0, 1536:2048]
        scan_keep = xin[:, 0, 0:WIDTH]
        logit = xin[:, 1, 0:WIDTH].rearrange("p (h t) -> p h t", h=G_HEADS)
        soft = xin[:, 1, WIDTH:2 * WIDTH].rearrange("p (h t) -> p h t", h=G_HEADS)
        merged = xin
        norm_rows = proj[0:16, 1, R_QK + P:R_QK + 2 * P]
        gain_rows = proj[0:28, 1, R_QK:R_QK + P]
        gateT = xin[0:G_RANK, 1, WIDTH:WIDTH + SEQ]
        ang = [head_a[:, n * SEQ:(n + 1) * SEQ] for n in range(6)]

        qn = [head_a[:, 0:256], head_b[:, 0:256]]
        qr = [head_a[0:ROPE, 256:512], head_b[0:ROPE, 256:512]]
        kn = [head_a[:, 512:768], head_b[:, 512:768]]
        vh = [a[:, 768:1024].rearrange("p (b d) -> p b d", b=TB) for a in (head_a, head_b)]
        sc = [head_a[:, 1024:1408], s_b]
        pT = [head_a[:, 1408:1792].rearrange("p (n q) -> p n q", n=3), head_pT_b]
        rope_tmp = kr_tok[:, :, :].rearrange("p b n -> p (b n)")[0:ROPE, 0:SEQ]

        g_state = proj[:, 0, R_ZA:R_ZA + 768].rearrange("p (n d) -> p n d", n=3)
        g_q_dec = proj[:, 0, R_ZA + 768:R_ZA + 1024]
        g_v = proj[:, 1, R_ZA:R_ZA + 512].rearrange("p (b d) -> p b d", b=TB)
        g_k_dec = proj[:, 1, R_ZA + 512:R_ZA + 768]
        g_k_end = proj[:, 1, R_ZA + 768:R_ZA + 1024]
        g_k_tok = head_a[:, 0:256].rearrange("p (b d) -> p b d", b=TB)
        g_att = head_a[:, 512:768].rearrange("p (b i) -> p b i", b=TB)
        g_junk = head_a[:, 1024:1280]

        acc = ctx.enter_context(nc.psum_tensor("acc", [P, 4, NCOL], F32))
        acc_a, acc_b = acc[:, 0:2, :], acc[:, 2:4, :]
        aux = [ctx.enter_context(nc.psum_tensor(f"aux{k}", [P, NCOL], F32)) for k in range(4)]

        x_landed = [sem(f"x_landed{k}") for k in range(4)]
        const_landed, gains_landed, pos_landed = sem("const_landed"), sem("gains_landed"), sem("pos_landed")
        norm_landed = sem("norm_landed")
        gains_turned, gains_done = sem("gains_turned"), sem("gains_done")
        band_landed, bias_landed, x_again, fnorm_landed = sem("band_landed"), sem("bias_landed"), sem("x_again"), sem("fnorm_landed")
        slot_landed = [sem(f"slot_landed{k}") for k in range(RING)]
        swap_landed = [sem("swap_landed0"), sem("swap_landed1")]
        kv_landed = [sem("kv_landed0"), sem("kv_landed1")]
        hi_ready, lo_ready, slot_used = sem("hi_ready"), sem("lo_ready"), sem("slot_used")
        aux_ready = sem("aux_ready")
        waited = sem("waited")
        aux_free = [sem(f"aux_free{k}") for k in range(4)]
        a_free, b_free = sem("a_free"), sem("b_free")
        x_ssq, x_ms, x_rstd = sem("x_ssq"), sem("x_ms"), sem("x_rstd")
        xT_hi_done, xT_lo_done = sem("xT_hi_done"), sem("xT_lo_done")
        pool_const, angle_step, angle_done, table_done = sem("pool_const"), sem("angle_step"), sem("angle_done"), sem("table_done")
        kr_done, krT_part, krT_done, gateT_done = sem("kr_done"), sem("krT_part"), sem("krT_done"), sem("gateT_done")
        c_ssq, c_ms, c_rstd, c_scaled = sem("c_ssq"), sem("c_ms"), sem("c_rstd"), sem("c_scaled")
        cT_hi_done, cT_lo_done = sem("cT_hi_done"), sem("cT_lo_done")
        logit_done, soft_arg, soft_exp, soft_done = sem("logit_done"), sem("soft_arg"), sem("soft_exp"), sem("soft_done")
        keep_set, log_a_done, bcum_done = sem("keep_set"), sem("log_a_done"), sem("bcum_done")
        mT_hi_done, mT_lo_done = sem("mT_hi_done"), sem("mT_lo_done")
        z_silu, yb_done, yb_hi_done, yb_lo_done, qkT_done = sem("z_silu"), sem("yb_done"), sem("yb_hi_done"), sem("yb_lo_done"), sem("qkT_done")
        zc_done = sem("zc_done")
        rope_part, qr_done, qn_done, kv_done = sem("rope_part"), sem("qr_done"), sem("qn_done"), sem("kv_done")
        s_done, m_done, p_done, inv_done = sem("s_done"), sem("m_done"), sem("p_done"), sem("inv_done")
        pT_done, ya_done, ya_hi_done, ya_lo_done = sem("pT_done"), sem("ya_done"), sem("ya_hi_done"), sem("ya_lo_done")
        bias_added, gate_done, gated, merged_done = sem("bias_added"), sem("gate_done"), sem("gated"), sem("merged_done")
        b_last_done, decays, g_v_done, g_dec_done = sem("b_last_done"), sem("decays"), sem("g_v_done"), sem("g_dec_done")
        att_copied, att_done, k_tok_done, state_step = sem("att_copied"), sem("att_done"), sem("k_tok_done"), sem("state_step")
        att_zero = sem("att_zero")
        o_ssq, o_ms, o_rstd, yc_done, yc_hi_done, yc_lo_done = sem("o_ssq"), sem("o_ms"), sem("o_rstd"), sem("yc_done"), sem("yc_hi_done"), sem("yc_lo_done")
        mg_hi_done, mg_lo_done = sem("mg_hi_done"), sem("mg_lo_done")
        res_done, f_ssq, f_sum, f_ms, f_rstd, f_done, stored = (sem("res_done"), sem("f_ssq"), sem("f_sum"), sem("f_ms"), sem("f_rstd"), sem("f_done"),
                                                        sem("stored"))

        def landed(s, i=0, per=0):
            return 16 + 16 * (s // RING) + (16 if s + (i * per if isinstance(i, int) else 0) >= S_SMALL else 0) + (per // RING) * 16 * i

        def apart(eng):
            eng.sem_inc(waited, 1)

        def aux_wait(eng, a, i=0, per=0):
            if a >= 4:
                eng.wait_ge(aux_free[a % 4], a // 4 + (per // 4) * i)

        pool_slot = {A_PW + n: S_ZC + k for n, k in enumerate([k for k, kind in enumerate(ZC_SLOTS) if kind == "p"])}
        head_slot = {A_B0 + n: S_B0 + 4 + n for n in range(4)}

        def counted(a):
            return a - sum(b < a for b in (*pool_slot, *head_slot)) - (12 if a >= A_B1 else 0)

        def task_wait(eng, a, i=0):
            if a in pool_slot:
                eng.wait_ge(slot_used, pool_slot[a] + 1)
            elif a in head_slot:
                eng.wait_ge(slot_used, head_slot[a] + 1 + 16 * i)
            else:
                eng.wait_ge(aux_ready, counted(a) + 1 + 8 * i)

        block = ctx.enter_context(nc.Block())

        @block.sync
        def _(sp):
            def load(s, dst_n, src, i=0, per=0, shape=None):
                if s >= RING:
                    sp.wait_ge(lo_ready, s - RING + 1 + per * i)
                    apart(sp)
                dst = raw[:, s % RING, 0:dst_n].rearrange("p (t n) -> p t n", t=shape)
                return sp.dma_start(dst, src)

            def load_chunk(s, src, col, k, i=0, per=0):
                load(s, SLOT, src[:, 2 * k:2 * k + 2, bass.ds(col, NCOL)], i, per, 2).then_inc(slot_landed[s % RING], 16)

            for c, col in enumerate((C_Q, C_KV)):
                for k in range(8):
                    if c == 0 and k < 4:
                        sp.dma_start(xin[:, :, k * NCOL:(k + 1) * NCOL], x_d[:, :, k * NCOL:(k + 1) * NCOL]).then_inc(x_landed[k], 16)
                    load_chunk(S_PROJ + 8 * c + k, w_in_d, col, k)
            task_wait(sp, A_X + 7)
            sp.wait_ge(x_ssq, 2)
            sp.dma_start(band, consts[:, K_BAND:K_END].rearrange("p (g t) -> p g t", g=4)).then_inc(band_landed, 16)
            sp.dma_start(w_gate, gla_w_gate[0]).then_inc(band_landed, 16)
            with sp.Fori(0, N_PAIRS - 1) as i:
                for c in range(2):
                    for k in range(8):
                        load_chunk(S_PROJ + 16 + 8 * c + k, w_in_d, C_ZA + c * NCOL + i * WIDTH, k, i, 16)
            for k in range(RING):
                s = S_SMALL + k
                sp.wait_ge(lo_ready, s - RING + 1)
                dst = raw[:, s % RING, 0:4 * 80].rearrange("p (t n) -> p t n", t=4)
                sp.dma_start(dst[:, :, 0:ROPE], w_in_d[:, 4 * k:4 * k + 4, C_KROPE:C_KROPE + ROPE]).then_inc(slot_landed[s % RING], 16)
                sp.dma_start(dst[:, :, ROPE:80], w_in_d[:, 4 * k:4 * k + 4, C_LR:C_LR + G_RANK]).then_inc(slot_landed[s % RING], 16)
            z = p = 0
            for k, kind in enumerate(ZC_SLOTS):
                if kind == "z":
                    load_chunk(S_ZC + k, w_in_d, C_ZC + NCOL * (z // 8), z % 8)
                    z += 1
                else:
                    load(S_ZC + k, 2 * 256, pool_w_d[p], shape=2).then_inc(slot_landed[(S_ZC + k) % RING], 16)
                    p += 1

            def load_turn(s0, per, n, gate_no, i, heads):
                gcol = C_GATES + n * D + i * NCOL
                for k in range(4):
                    load_chunk(s0 + k, w_in_d, gcol, k, i, per)
                task_wait(sp, A_QK + 3)
                sp.wait_ge(b_free, gate_no + 8 + i)
                apart(sp)
                sp.dma_start(bias_row, b_merge[0, n, bass.ds(i * NCOL, NCOL)].partition_broadcast(P)).then_inc(bias_landed, 16)
                k = 4
                if heads:
                    for j in range(2):
                        s, h = s0 + 4 + 2 * j, 2 * i + j
                        col = h * (NOPE + ROPE)
                        sp.wait_ge(lo_ready, s - RING + 1 + per * i)
                        apart(sp)
                        dst = raw[:, s % RING, :].rearrange("p (t n) -> p t n", t=4)
                        sp.dma_start(dst[:, :, 0:192], w_uq_d[:, :, bass.ds(col, 192)]).then_inc(slot_landed[s % RING], 16)
                        sp.dma_start(dst[:, :, 192:224], w_uq_d[:, :, bass.ds(col + 160, 32)]).then_inc(swap_landed[j], 16)
                        sp.dma_start(dst[:, :, 224:256], w_uq_d[:, :, bass.ds(col + 128, 32)]).then_inc(swap_landed[j], 16)
                        sp.wait_ge(lo_ready, s + 1 - RING + 1 + per * i)
                        apart(sp)
                        dst = raw[:, (s + 1) % RING, :].rearrange("p (t h n) -> p t h n", t=4, h=2)
                        for n, landed_ in enumerate((slot_landed[(s + 1) % RING], kv_landed[j])):
                            sp.dma_start(dst[:, :, n, :], w_ukv_d[:, :, 2 * i + n, j, :]).then_inc(landed_, 16)
                    k = 8
                for g in range(4, 8):
                    load_chunk(s0 + k, w_in_d, gcol, g, i, per)
                    k += 1
                for g in range(4):
                    load_chunk(s0 + k, w_branch_d[n], i * NCOL, g, i, per)
                    k += 1

            with sp.Fori(0, 4) as i:
                load_turn(S_B0, 16, 1, 0, i, True)
            with sp.Fori(0, 4) as i:
                load_turn(S_B1, 12, 0, 4, i, False)
            with sp.Fori(0, 4) as i:
                load_turn(S_B2, 12, 2, 8, i, False)
            sp.wait_ge(slot_used, S_B2 + 12)
            sp.dma_start(x_res, x_d).then_inc(x_again, 16)
            sp.dma_start(fnorm_row, final_norm.partition_broadcast(P)).then_inc(fnorm_landed, 16)
            with sp.Fori(0, 2) as i:
                for c in range(2):
                    for k in range(8):
                        load_chunk(S_OUT + 8 * c + k, w_out_d, c * NCOL + i * WIDTH, k, i, 16)
            for q in range(4):
                tb, half = q // 2, q % 2
                sp.wait_ge(f_done, q + 1)
                sp.dma_start(out_d[:, tb, half * WIDTH:(half + 1) * WIDTH], x_res[:, tb, half * WIDTH:(half + 1) * WIDTH]).then_inc(stored, 16)
            sp.wait_ge(stored, 64)

        @block.gpsimd
        def _(pool):
            nc.gpsimd.memset(minus_half, -0.5).then_inc(pool_const, 1)
            pool.wait_ge(pool_const, 1)

            def inv_root(out_, ssq, n, of, ready, at, mid, done, at_mid):
                pool.wait_ge(ready, at)
                apart(pool)
                nc.gpsimd.tensor_scalar(ms_tmp[:, 0:n], ssq, 1.0 / of, EPS, ALU.mult, ALU.add).then_inc(mid, 1)
                pool.wait_ge(mid, at_mid)
                nc.gpsimd.tensor_tensor(out_, ms_tmp[:, 0:n], minus_half[:, 0:n], ALU.pow).then_inc(done, 1)

            inv_root(rstd_x, ssq_x, 2, D, x_ssq, 2, x_ms, x_rstd, 1)

            count = [0]

            def step(ins):
                count[0] += 1
                ins.then_inc(angle_step, 1)
                pool.wait_ge(angle_step, count[0])

            def ts(o, i0, s0, s1, op0, op1=None):
                if op1 is None:
                    step(nc.gpsimd.tensor_scalar(o, i0, s0, None, op0))
                else:
                    step(nc.gpsimd.tensor_scalar(o, i0, s0, s1, op0, op1))

            def tt(o, i0, i1, op):
                step(nc.gpsimd.tensor_tensor(o, i0, i1, op))

            pos_i, a, part, t, r, turns = ang[0].bitcast(I32), ang[1], ang[2], ang[3], ang[4], ang[5]
            pool.wait_ge(pos_landed, 16)
            pool.wait_ge(const_landed, 16)
            step(nc.gpsimd.tensor_copy(a, pos_i))
            ts(a, a, const[:, K_FREQ:K_FREQ + 1], None, ALU.mult)
            step(nc.gpsimd.memset(turns, 0.0))
            for scale, top, low in TURNS:
                ts(part, a, 1.0 / scale, M_RNE, ALU.mult, ALU.add)
                ts(part, part, M_RNE, None, ALU.subtract)
                ts(t, part, -scale, None, ALU.mult)
                tt(a, a, t, ALU.add)
                ts(t, part, top, None, ALU.mult)
                ts(r, t, M_RNE, None, ALU.add)
                ts(r, r, M_RNE, None, ALU.subtract)
                tt(t, t, r, ALU.subtract)
                tt(turns, turns, t, ALU.add)
                ts(t, part, low, None, ALU.mult)
                tt(turns, turns, t, ALU.add)

            def reduce(v):
                ts(part, v, 1.0 / TWO_PI, M_RNE, ALU.mult, ALU.add)
                ts(part, part, M_RNE, None, ALU.subtract)
                for p_i in (PI1, PI2, PI3):
                    ts(t, part, -p_i, None, ALU.mult)
                    tt(v, v, t, ALU.add)

            reduce(a)
            ts(r, turns, M_RNE, None, ALU.add)
            ts(r, r, M_RNE, None, ALU.subtract)
            tt(turns, turns, r, ALU.subtract)
            ts(t, turns, float(np.float32(TWO_PI)), None, ALU.mult)
            tt(a, a, t, ALU.add)
            reduce(a)
            lim = 3.1415925
            ts(a, a, lim, -lim, ALU.min, ALU.max)
            ts(t, a, 0.0, 2.0, ALU.max, ALU.mult)
            tt(t, t, a, ALU.subtract)
            ts(rope_tab[0:64, :], t[0:64], -1.0, float(np.float32(np.pi / 2)), ALU.mult, ALU.add)
            nc.gpsimd.tensor_scalar(rope_tab[64:128, :], a[64:128], const[64:128, K_SIGN:K_SIGN + 1], None, ALU.mult).then_inc(angle_done, 1)

            pool.wait_ge(angle_done, 1)
            inv_root(rstd_c, ssq_c, 4, LORA, c_ssq, 4, c_ms, c_rstd, 1)

            with pool.Fori(0, 4) as i:
                pool.wait_ge(att_copied, 2 * i + 2)
                apart(pool)
                nc.gpsimd.affine_select(out=g_att, in_=g_att, compare_op=ALU.is_ge, fill=0.0, base=0,
                                        pattern=[[0, TB], [1, P]], channel_multiplier=-1).then_inc(att_done, 1)
                inv_root(rstd_o, ssq_o, 2, G_DV, o_ssq, 2 * i + 2, o_ms, o_rstd, i + 1)
            inv_root(rstd_f, ssq_ft, 2, D, f_sum, 1, f_ms, f_rstd, 1)

        @block.tensor
        def _(pe):
            mm = nc.tensor.matmul

            def mm3(o, s_hi, s_lo, m_hi, m_lo, start, stop):
                mm(o, s_hi, m_hi, start=start, stop=False)
                mm(o, s_hi, m_lo, start=False, stop=False)
                return mm(o, s_lo, m_hi, start=False, stop=stop)

            def rows(s_hi, s_lo, acc_x, s, kts, n_kt, i=0, per=0, width=NCOL):
                pe.wait_ge(lo_ready, s + 1 + per * i)
                k = s % RING
                for n, kt in enumerate(kts):
                    for tb in range(TB):
                        cols, tok = slice(n * width, (n + 1) * width), slice(tb * P, (tb + 1) * P)
                        last = mm3(acc_x[:, tb, 0:width], s_hi[:, kt, tok], s_lo[:, kt, tok],
                                   w_hi[:, k, cols], w_lo[:, k, cols], kt == 0, kt == n_kt - 1)
                return last

            def chunk_slot(s, k, acc_x, free, free_at, i=0, per=0, s_hi=xT_hi, s_lo=xT_lo, n_slots=8):
                if k == 0:
                    pe.wait_ge(free, free_at)
                rows(s_hi, s_lo, acc_x, s, (2 * k, 2 * k + 1), 2 * n_slots, i, per).then_inc(slot_used, 1)

            def transposes(a, pairs, i=0, per=0):
                aux_wait(pe, a, i, per)
                for o, src in pairs:
                    last = nc.tensor.transpose(o, src, ident[0:src.shape[0], 0:src.shape[0]])
                last.then_inc(aux_ready, 1)

            def first_slot(k):
                pe.wait_ge(xT_lo_done, 2 * k + 2)
                chunk_slot(S_PROJ + k, k, acc_a, a_free, 1)

            pe.wait_ge(const_landed, 16)
            for a in range(8):
                pe.wait_ge(x_landed[a // 2], 16)
                if a >= 4:
                    first_slot(a - 4)
                transposes(A_X + a, [(aux[a % 4][:, (2 * n + tb) * P:(2 * n + tb + 1) * P],
                                      xin[:, tb, (2 * a + n) * P:(2 * a + n + 1) * P]) for n in range(2) for tb in range(TB)])
                if a == 0:
                    pe.wait_ge(norm_landed, 16)
                    nc.tensor.transpose(acc_a[:, 0, 0:16], norm_rows, ident[0:16, 0:16]).then_inc(gains_turned, 1)
                if a == 3:
                    pe.wait_ge(gains_landed, 80)
                    nc.tensor.transpose(acc_b[:, 0, 0:28], gain_rows, ident[0:28, 0:28]).then_inc(gains_turned, 1)
            for k in range(4, 8):
                first_slot(k)
            for k in range(8):
                chunk_slot(S_PROJ + 8 + k, k, acc_b, b_free, 1)
            with pe.Fori(0, N_PAIRS - 1) as i:
                for k in range(8):
                    chunk_slot(S_PROJ + 16 + k, k, acc_a, a_free, i + 2, i, 16)
                for k in range(8):
                    chunk_slot(S_PROJ + 24 + k, k, acc_b, b_free, i + 2, i, 16)
            pe.wait_ge(a_free, N_PAIRS + 1)
            for k in range(RING):
                rows(xT_hi, xT_lo, acc_a, S_SMALL + k, range(4 * k, 4 * k + 4), KT, width=80).then_inc(slot_used, 1)

            def small_task(a):
                bank = aux[a % 4]
                if a == A_KR:
                    pe.wait_ge(kr_done, 8)
                    transposes(a, [(bank[:, tb * P:(tb + 1) * P], kr_tok[:, tb, 0:P]) for tb in range(TB)])
                elif a == A_GT:
                    transposes(a, [(bank[0:G_RANK, tb * P:(tb + 1) * P], kr_tok[:, tb, P:P + G_RANK]) for tb in range(TB)])
                elif a < A_LG:
                    n0 = 2 * (a - A_CT)
                    pe.wait_ge(c_scaled, 4)
                    transposes(a, [(bank[:, (2 * n + tb) * P:(2 * n + tb + 1) * P], c_tok[:, tb, (n0 + n) * P:(n0 + n + 1) * P])
                                   for n in range(2) for tb in range(TB)])
                elif a < A_BAND:
                    aux_wait(pe, a)
                    pe.wait_ge(gateT_done, 1)
                    pe.wait_ge(band_landed, 32)
                    for n in range(2):
                        h = 2 * (a - A_LG) + n
                        last = mm(bank[:, n * SEQ:(n + 1) * SEQ], w_gate[:, h * G_DK:(h + 1) * G_DK], gateT, start=True, stop=True)
                    last.then_inc(aux_ready, 1)
                elif a < A_PW:
                    g = a - A_BAND
                    aux_wait(pe, a)
                    for n in range(2):
                        col = g * 256 + n * P
                        mm(bank[:, n * SEQ:(n + 1) * SEQ], u_tok[:, 0, col:col + P], band[:, g, 0:SEQ], start=True, stop=False)
                        last = mm(bank[:, n * SEQ + P:(n + 1) * SEQ], u_tok[:, 1, col:col + P], band[:, g, SEQ:SEQ + P], start=False, stop=True)
                    last.then_inc(aux_ready, 1)
                elif a < A_YB:
                    g = a - A_PW
                    s = S_ZC + [k for k, kind in enumerate(ZC_SLOTS) if kind == "p"][g]
                    aux_wait(pe, a)
                    pe.wait_ge(mT_lo_done, g + 1)
                    pe.wait_ge(lo_ready, s + 1)
                    for tb in range(TB):
                        for kt in range(2):
                            tok, cols = slice(tb * P, (tb + 1) * P), slice(kt * 256, (kt + 1) * 256)
                            last = mm3(bank[:, tb * 256:(tb + 1) * 256], y1_hi[:, 2 * g + kt, tok], y1_lo[:, 2 * g + kt, tok],
                                       w_hi[:, s % RING, cols], w_lo[:, s % RING, cols], kt == 0, kt == 1)
                    last.then_inc(slot_used, 1)
                elif a < A_QK:
                    g = a - A_YB
                    pe.wait_ge(yb_done, g + 1)
                    transposes(a, [(bank[:, (2 * n + tb) * P:(2 * n + tb + 1) * P], zb[:, tb, (2 * g + n) * P:(2 * g + n + 1) * P])
                                   for n in range(2) for tb in range(TB)])
                else:
                    n0 = 2 * (a - A_QK)
                    transposes(a, [(bank[:, (2 * n + tb) * P:(2 * n + tb + 1) * P], proj[:, tb, R_QK + (n0 + n) * P:R_QK + (n0 + n + 1) * P])
                                   for n in range(2) for tb in range(TB)])

            z = 0
            for k, kind in enumerate(ZC_SLOTS):
                if kind == "z":
                    acc_x, free, at = ((acc_b, b_free, 7), (acc_a, a_free, 8))[z // 8]
                    chunk_slot(S_ZC + k, z % 8, acc_x, free, at)
                    z += 1
                for a in ZC_TASKS.get(k, ()):
                    small_task(a)

            def gate_slot(s, k, n_gate, i, per):
                chunk_slot(s, k, acc_b, b_free, n_gate + 8 + i, i, per)

            def branch_slot(s, k, n_gate, i, per, y_hi, y_lo):
                chunk_slot(s, k, acc_a, a_free, n_gate + 9 + i, i, per, y_hi, y_lo, 4)

            with pe.Fori(0, 4) as i:
                def at(k):
                    return aux[(A_B0 + k) % 4], A_B0 + k
                for k in range(4):
                    gate_slot(S_B0 + k, k, 0, i, 16)
                pe.wait_ge(yb_lo_done, 8)
                for j in range(2):
                    s = S_B0 + 4 + 2 * j
                    bank, a = at(2 * j)
                    pe.wait_ge(lo_ready, s + 1 + 16 * i)
                    pe.wait_ge(cT_lo_done, 8)
                    aux_wait(pe, a, i, 12)
                    for part_ in range(2):
                        for kt in range(4):
                            cols = slice(kt * 256 + part_ * P, kt * 256 + part_ * P + P)
                            last = mm3(bank[:, part_ * SEQ:(part_ + 1) * SEQ], w_hi[:, s % RING, cols], w_lo[:, s % RING, cols],
                                       cT_hi[:, kt, :], cT_lo[:, kt, :], kt == 0, kt == 3)
                    last.then_inc(slot_used, 1)
                    s += 1
                    bank, a = at(2 * j + 1)
                    pe.wait_ge(lo_ready, s + 1 + 16 * i)
                    aux_wait(pe, a, i, 12)
                    for n in range(2):
                        for kt in range(4):
                            if j == 0:
                                cols = slice(kt * 256 + n * P, kt * 256 + (n + 1) * P)
                                last = mm3(bank[:, n * SEQ:(n + 1) * SEQ], w_hi[:, s % RING, cols], w_lo[:, s % RING, cols],
                                           cT_hi[:, 4 + kt, :], cT_lo[:, 4 + kt, :], kt == 0, kt == 3)
                            else:
                                cols, tok = slice(kt * 256, (kt + 1) * 256), slice(n * P, (n + 1) * P)
                                last = mm3(bank[:, n * SEQ:(n + 1) * SEQ], cT_hi[:, 4 + kt, tok], cT_lo[:, 4 + kt, tok],
                                           w_hi[:, s % RING, cols], w_lo[:, s % RING, cols], kt == 0, kt == 3)
                    last.then_inc(slot_used, 1)

                def head_scores(j):
                    bank, a = at(4 + j)
                    aux_wait(pe, a, i, 12)
                    pe.wait_ge(krT_done, 1)
                    pe.wait_ge(qr_done, 2 * i + j + 1)
                    pe.wait_ge(qn_done, 2 * i + j + 1)
                    pe.wait_ge(kv_done, 4 * i + j + 1)
                    for tb, lo, hi in ((0, 0, 128), (1, 128, 384)):
                        tok = slice(tb * P, (tb + 1) * P)
                        mm(bank[:, lo:hi], qn[j][:, tok], kn[j][:, 0:hi - lo], start=True, stop=False)
                        last = mm(bank[:, lo:hi], qr[j][:, tok], krT[:, 0:hi - lo], start=False, stop=True)
                    last.then_inc(aux_ready, 1)

                def head_p(j):
                    bank, a = at(6 + j)
                    pe.wait_ge(p_done, 2 * (2 * i + j + 1))
                    transposes(a, [(bank[:, n * P:(n + 1) * P], sc[j][:, n * P:(n + 1) * P]) for n in range(3)], i, 12)

                def head_o(j):
                    bank, a = at(8 + j)
                    aux_wait(pe, a, i, 12)
                    pe.wait_ge(pT_done, 2 * i + j + 1)
                    pe.wait_ge(kv_done, 4 * i + 3 + j)
                    mm(bank[:, 0:P], pT[j][:, 0, :], vh[j][:, 0, :], start=True, stop=True)
                    mm(bank[:, P:2 * P], pT[j][:, 1, :], vh[j][:, 0, :], start=True, stop=False)
                    mm(bank[:, P:2 * P], pT[j][:, 2, :], vh[j][:, 1, :], start=False, stop=True).then_inc(aux_ready, 1)

                def head_y(j):
                    bank, a = at(10 + j)
                    pe.wait_ge(ya_done, 2 * (2 * i + j + 1))
                    transposes(a, [(bank[:, tb * P:(tb + 1) * P], yh[:, tb, j * P:(j + 1) * P]) for tb in range(TB)], i, 12)

                for k, work in enumerate((head_scores, head_p)):
                    for j in range(2):
                        gate_slot(S_B0 + 8 + 2 * k + j, 4 + 2 * k + j, 0, i, 16)
                        work(j)
                for k, work in enumerate((head_o, head_y)):
                    for j in range(2):
                        branch_slot(S_B0 + 12 + 2 * k + j, 2 * k + j, 0, i, 16, y0_hi, y0_lo)
                        work(j)

            with pe.Fori(0, 4) as i:
                def g_bank(k):
                    aux_wait(pe, A_B1 + k, i, 8)
                    return aux[(A_B1 + k) % 4]

                for k in range(12):
                    if k < 8:
                        gate_slot(S_B1 + k, k, 4, i, 12)
                    else:
                        if k == 8:
                            pe.wait_ge(ya_lo_done, HEADS)
                        branch_slot(S_B1 + k, k - 8, 4, i, 12, y1_hi, y1_lo)
                    if k == 1:
                        bank = g_bank(0)
                        pe.wait_ge(g_dec_done, 3 * i + 2)
                        for tb in range(TB):
                            tok = slice(tb * P, (tb + 1) * P)
                            last = mm(bank[:, tok], g_k_dec[:, tok], g_q_dec[:, tok], start=True, stop=True)
                        last.then_inc(aux_ready, 1)
                    if k == 2:
                        pe.wait_ge(g_dec_done, 3 * i + 3)
                        transposes(A_B1 + 1, [(aux[(A_B1 + 1) % 4][:, tb * P:(tb + 1) * P], g_k_end[:, tb * P:(tb + 1) * P]) for tb in range(TB)], i, 8)
                    if k == 4:
                        pe.wait_ge(k_tok_done, i + 1)
                        pe.wait_ge(g_v_done, i + 1)
                        for t_, chunks in ((2, (0, 2)), (3, (1,))):
                            bank = g_bank(t_)
                            for n, c in enumerate(chunks):
                                r0 = CHUNK * (c % 2)
                                last = mm(bank[:, n * G_DV:(n + 1) * G_DV], g_k_tok[r0:r0 + CHUNK, c // 2, :],
                                          g_v[r0:r0 + CHUNK, c // 2, :], start=True, stop=True)
                            last.then_inc(aux_ready, 1)
                    if k == 6:
                        pe.wait_ge(att_done, i + 1)
                        pe.wait_ge(state_step, 3 * i + 3)
                        for tb in range(TB):
                            bank = g_bank(4 + tb)
                            last = mm(bank[:, 0:G_DV], g_att[:, tb, :], g_v[:, tb, :], start=True, stop=True)
                            for c in (2 * tb, 2 * tb + 1):
                                if c:
                                    r0 = CHUNK * (c % 2)
                                    last = mm(bank[r0:r0 + CHUNK, 0:G_DV], g_q_dec[:, c * CHUNK:(c + 1) * CHUNK],
                                              g_state[:, c - 1, :], start=False, stop=True, skip_group_check=True)
                            last.then_inc(aux_ready, 1)
                    if k == 9:
                        pe.wait_ge(yc_done, 2 * i + 2)
                        for n in range(2):
                            a = A_B1 + 6 + n
                            transposes(a, [(aux[a % 4][:, tb * P:(tb + 1) * P], yh[:, tb, n * P:(n + 1) * P]) for tb in range(TB)], i, 8)

            def merge_turn(k, i):
                if k < 8:
                    gate_slot(S_B2 + k, k, 8, i, 12)
                else:
                    if k == 8:
                        pe.wait_ge(yc_lo_done, 8)
                    branch_slot(S_B2 + k, k - 8, 8, i, 12, y0_hi, y0_lo)

            def merged_task(n, after):
                pe.wait_ge(merged_done, after)
                transposes(A_MT + n, [(aux[n % 4][:, (2 * m + tb) * P:(2 * m + tb + 1) * P],
                                       merged[:, tb, (2 * n + m) * P:(2 * n + m + 1) * P]) for m in range(2) for tb in range(TB)])

            with pe.Fori(0, 3) as i:
                for k in range(12):
                    merge_turn(k, i)
            for k in range(12):
                merge_turn(k, 3)
                if 8 <= k <= 10:
                    for n in range(2 * (k - 8), 2 * (k - 8) + 2):
                        merged_task(n, 11)
            for n in (6, 7):
                merged_task(n, 12)

            with pe.Fori(0, 2) as i:
                for c, (acc_x, free) in enumerate(((acc_b, b_free), (acc_a, a_free))):
                    for k in range(8):
                        pe.wait_ge(mg_lo_done, k + 1)
                        chunk_slot(S_OUT + 8 * c + k, k, acc_x, free, 20 + c + i, i, 16)

        @block.scalar
        def _(act):
            fn = nc.scalar.activation

            def hi(s, i=0, per=0, n=SLOT):
                k = s % RING
                act.wait_ge(slot_landed[k], landed(s, i, per))
                if s >= RING:
                    act.wait_ge(slot_used, s - RING + 1 + per * i)
                fn(w_hi[:, k, 0:n], raw[:, k, 0:n], ACT.Copy).then_inc(hi_ready, 1)

            act.dma_start(norm_rows, norm_g[0].rearrange("(t p) -> t p", p=P)).then_inc(norm_landed, 16)
            act.dma_start(const[:, :], consts[:, 0:K_BAND]).then_inc(const_landed, 16)
            row = 0
            for src in (mla_q_norm, mla_kv_norm, pool_scale, gla_norm, gla_b_gate):
                n = src.shape[1] // P
                act.dma_start(gain_rows[row:row + n, :], src[0].rearrange("(t p) -> t p", p=P)).then_inc(gains_landed, 16)
                row += n
            act.dma_start(ang[0].bitcast(I32), positions[0].partition_broadcast(P)).then_inc(pos_landed, 16)
            act.wait_ge(pool_const, 1)
            fn(stat[:, 63:64], minus_half[:, 0:1], ACT.Copy)
            act.wait_ge(gains_done, 1)
            for kt in range(KT):
                task_wait(act, A_X + kt // 2)
                fn(xT_hi[:, kt, :], aux[(kt // 2) % 4][:, (kt % 2) * SEQ:(kt % 2 + 1) * SEQ], ACT.Copy, scale=g_norm[:, kt:kt + 1]).then_inc(xT_hi_done, 1)
                if kt % 2 == 1:
                    hi(S_PROJ + kt // 2)

            def pair(i, first=False, last=False):
                for k in range(16):
                    if first and k in (2, 3):
                        tb = k - 2
                        fn(proj[:, tb, 2 * WIDTH:2 * WIDTH + D], xin[:, tb, :], ACT.Square, accum_out=ssq_x[:, tb:tb + 1]).then_inc(x_ssq, 1)
                    if first and k == 7:
                        act.wait_ge(x_rstd, 1)
                        act.wait_ge(x_ssq, 2)
                    if k == 7 or k == 15:
                        c, acc_x, free = ((0, acc_a, a_free), (1, acc_b, b_free))[k // 8]
                        act.wait_ge(slot_used, S_PROJ + k + 1 + 16 * i)
                        fn(proj[:, 0, bass.ds(i * WIDTH + c * NCOL, NCOL)], acc_x[:, 0, :], ACT.Copy, scale=rstd_x[:, 0:1])
                        fn(proj[:, 1, bass.ds(i * WIDTH + c * NCOL, NCOL)], acc_x[:, 1, :], ACT.Copy, scale=rstd_x[:, 1:2]).then_inc(free, 1)
                    if k >= 4 or not first:
                        hi(S_PROJ + 4 + k, i, 16, 320 if last and k >= 12 else SLOT)

            pair(0, first=True)
            with act.Fori(1, N_PAIRS - 1) as i:
                pair(i)
            pair(N_PAIRS - 1, last=True)
            for k in range(RING):
                hi(S_ZC + k)

            for c in range(2):
                for tb in range(TB):
                    if 2 * c + tb:
                        act.wait_ge(c_ssq, 2 * c + tb)
                    fn(xin[:, 1, 1536:2048], c_tok[:, tb, c * LORA:(c + 1) * LORA], ACT.Square,
                       accum_out=ssq_c[:, 2 * c + tb:2 * c + tb + 1]).then_inc(c_ssq, 1)

            def small_evac(a):
                bank = aux[a % 4]
                if a == A_GT:
                    task_wait(act, a)
                    fn(gateT, bank[0:G_RANK, 0:SEQ], ACT.Copy).then_inc(gateT_done, 1)
                elif A_CT <= a < A_LG:
                    task_wait(act, a)
                    for n in range(2):
                        kt = 2 * (a - A_CT) + n
                        fn(cT_hi[:, kt, :], bank[:, n * SEQ:(n + 1) * SEQ], ACT.Copy,
                           scale=(g_q if kt < 4 else g_kv)[:, kt % 4:kt % 4 + 1]).then_inc(cT_hi_done, 1)
                elif A_BAND <= a < A_PW:
                    task_wait(act, a)
                    g = a - A_BAND
                    fn(y1_hi[:, 2 * g:2 * g + 2, :].rearrange("p n t -> p (n t)"), bank[:, :], ACT.Copy).then_inc(mT_hi_done, 1)
                elif A_YB <= a < A_QK:
                    task_wait(act, a)
                    for n in range(2):
                        f = 2 * (a - A_YB) + n
                        fn(y0_hi[:, f, :], bank[:, n * SEQ:(n + 1) * SEQ], ACT.Copy, scale=g_pool[:, f:f + 1]).then_inc(yb_hi_done, 1)
                elif a >= A_QK:
                    task_wait(act, a)
                    n0 = 2 * (a - A_QK)
                    dst = (qT_all if n0 < 4 else kT_all)[:, n0 % 4:n0 % 4 + 2, :].rearrange("p h t -> p (h t)")
                    fn(dst, bank[:, :], ACT.Copy).then_inc(aux_free[a % 4], 1)

            z = 0
            for k, kind in enumerate(ZC_SLOTS):
                for a in ZC_TASKS.get(k, ()):
                    small_evac(a)
                if k == 1:
                    fn(zb, zb, ACT.Silu).then_inc(z_silu, 1)
                    act.wait_ge(angle_done, 1)
                    fn(rope_tab[:, :], rope_tab[:, :], ACT.Sin).then_inc(table_done, 1)
                if k == 3:
                    fn(za, za, ACT.Silu).then_inc(z_silu, 1)
                if kind == "z":
                    z += 1
                    if z % 8 == 0:
                        c, acc_x, free = ((0, acc_b, b_free), (1, acc_a, a_free))[z // 8 - 1]
                        act.wait_ge(slot_used, S_ZC + k + 1)
                        task_wait(act, A_LG - 1)
                        for tb in range(TB):
                            ins = fn(zc[:, tb, c * NCOL:(c + 1) * NCOL], acc_x[:, tb, :], ACT.Silu, scale=rstd_x[:, tb:tb + 1])
                        ins.then_inc(free, 1)
                nxt = S_ZC + k + RING
                hi(nxt, n=SLOT if k + RING >= len(ZC_SLOTS) or ZC_SLOTS[k + RING] == "z" else 512)
            act.wait_ge(soft_arg, 1)
            fn(soft, soft, ACT.Exp).then_inc(soft_exp, 1)
            act.wait_ge(soft_exp, 1)
            fn(soft, soft, ACT.Ln, bias=1.0).then_inc(soft_done, 1)

            def tanh_gate(n):
                act.wait_ge(bias_added, 2 * n + 2)
                fn(gate, gate, ACT.Tanh, scale=0.5).then_inc(gate_done, 1)

            scale = float(NOPE + ROPE) ** -0.5
            with act.Fori(0, 4) as i:
                for k in range(16):
                    j = k % 2
                    h1 = 2 * i + j + 1
                    if k in (4, 6):
                        j = (k - 4) // 2
                        act.wait_ge(rope_part, 2 * (2 * i + j + 1))
                        fn(qn[j], aux[(A_B0 + 2 * j) % 4][:, 0:SEQ], ACT.Copy).then_inc(qn_done, 1)
                    if k in (5, 7):
                        j = (k - 5) // 2
                        bank = aux[(A_B0 + 2 * j + 1) % 4]
                        task_wait(act, A_B0 + 2 * j + 1, i)
                        for n in range(2):
                            if j == 0:
                                fn(kn[n], bank[:, n * SEQ:(n + 1) * SEQ], ACT.Copy).then_inc(kv_done, 1)
                            else:
                                fn(vh[n], bank[:, :].rearrange("p (b h d) -> p b h d", b=TB, h=2)[:, :, n, :], ACT.Copy).then_inc(kv_done, 1)
                    if k in (8, 9):
                        act.wait_ge(m_done, 2 * i + j + 1)
                        for tb, lo, hi_ in ((0, 0, 128), (1, 128, 384)):
                            fn(sc[j][:, lo:hi_], sc[j][:, lo:hi_], ACT.Exp, bias=neg_m[j][:, tb:tb + 1], scale=scale,
                               accum_out=row_sum[j][:, tb:tb + 1]).then_inc(p_done, 1)
                    if k in (10, 11):
                        bank = aux[(A_B0 + 6 + j) % 4]
                        task_wait(act, A_B0 + 6 + j, i)
                        fn(pT[j].rearrange("p n q -> p (n q)"), bank[:, 0:384], ACT.Copy).then_inc(pT_done, 1)
                    if k == 11:
                        tanh_gate(i)
                    if k in (14, 15):
                        task_wait(act, A_B0 + 10 + j, i)
                        fn(y1_hi[:, bass.ds(2 * i + j, 1), :].rearrange("p n t -> p (n t)"), aux[(A_B0 + 10 + j) % 4][:, 0:SEQ], ACT.Copy).then_inc(ya_hi_done, 1)
                    if k == 0:
                        act.wait_ge(swap_landed[0], 32 * i + 32)
                    if k == 2:
                        act.wait_ge(swap_landed[1], 32 * i + 32)
                    if k in (1, 3):
                        act.wait_ge(kv_landed[k // 2], 16 * i + 16)
                    hi(S_B0 + k + RING, i, 16)

            with act.Fori(0, 4) as i:
                for k in range(12):
                    if k == 0:
                        act.wait_ge(b_last_done, i + 1)
                        head = bcum[:, bass.ds(i, 1), :].rearrange("p h t -> p (h t)")
                        fn(g_q_dec, head, ACT.Exp, scale=1.0 / G_TAU).then_inc(decays, 1)
                        fn(g_k_dec, head, ACT.Exp, scale=-1.0 / G_TAU).then_inc(decays, 1)
                        for c in range(4):
                            cols = slice(c * CHUNK, (c + 1) * CHUNK)
                            ins = fn(g_k_end[:, cols], bcum[:, bass.ds(i, 1), cols].rearrange("p h t -> p (h t)"), ACT.Exp,
                                     scale=-1.0 / G_TAU, bias=b_last[:, c:c + 1])
                        ins.then_inc(decays, 1)
                        fn(decay, b_last, ACT.Exp).then_inc(decays, 1)
                        fn(g_v, v_tok[:, :, bass.ds(i * G_DV, G_DV)], ACT.Copy).then_inc(g_v_done, 1)
                    if k == 6:
                        for tb in range(TB):
                            task_wait(act, A_B1 + 4 + tb, i)
                            if tb:
                                act.wait_ge(o_ssq, 2 * i + 1)
                            fn(g_junk, aux[(A_B1 + 4 + tb) % 4][:, 0:G_DV], ACT.Square, accum_out=ssq_o[:, tb:tb + 1]).then_inc(o_ssq, 1)
                    if k == 7:
                        tanh_gate(4 + i)
                    if k == 9:
                        for n in range(2):
                            task_wait(act, A_B1 + 6 + n, i)
                            fn(y0_hi[:, bass.ds(2 * i + n, 1), :].rearrange("p n t -> p (n t)"), aux[(A_B1 + 6 + n) % 4][:, 0:SEQ], ACT.Copy,
                               scale=g_gla[:, bass.ds(2 * i + n, 1)]).then_inc(yc_hi_done, 1)
                    hi(S_B1 + k + RING, i, 12)

            def merged_hi(n):
                task_wait(act, A_MT + n)
                if n == 0:
                    act.wait_ge(slot_used, S_B2 + 36 + 8)
                fn(xT_hi[:, 2 * n:2 * n + 2, :].rearrange("p n t -> p (n t)"), aux[n % 4][:, :], ACT.Copy, scale=0.5).then_inc(mg_hi_done, 1)

            with act.Fori(0, 3) as i:
                for k in range(12):
                    if k == 7:
                        tanh_gate(8 + i)
                    hi(S_B2 + k + RING, i, 12)
            for k in range(12):
                if k == 7:
                    tanh_gate(11)
                if 8 <= k <= 10:
                    merged_hi(2 * (k - 8))
                    merged_hi(2 * (k - 8) + 1)
                hi(S_B2 + 36 + k + RING)
            for n in (6, 7):
                merged_hi(n)

            for k in range(32):
                if k % 8 == 7:
                    c = k // 8
                    act.wait_ge(res_done, c + 1)
                    for tb in range(TB):
                        if 2 * c + tb:
                            act.wait_ge(f_ssq, 2 * c + tb)
                        fn(proj[:, 1, R_V:R_V + NCOL], x_res[:, tb, c * NCOL:(c + 1) * NCOL], ACT.Square,
                           accum_out=ssq_f[:, 4 * tb + c:4 * tb + c + 1]).then_inc(f_ssq, 1)
                if S_OUT + k + RING < S_END:
                    hi(S_OUT + k + RING)

        @block.vector
        def _(dve):
            v = nc.vector

            def lo(s, i=0, per=0, n=SLOT):
                k = s % RING
                dve.wait_ge(hi_ready, s + 1 + per * i)
                v.tensor_tensor(w_lo[:, k, 0:n], raw[:, k, 0:n], w_hi[:, k, 0:n].bitcast(F32), ALU.subtract).then_inc(lo_ready, 1)

            def lo_of(dst, bank, scale_, hi_):
                return v.scalar_tensor_tensor(out=dst, in0=bank, scalar=scale_, in1=hi_.bitcast(F32), op0=ALU.mult, op1=ALU.subtract)

            dve.wait_ge(gains_turned, 1)
            v.tensor_copy(gains[:, 0:16], acc_a[:, 0, 0:16]).then_inc(gains_done, 1)
            dve.wait_ge(gains_done, 1)
            v.memset(stat[:, 60:61], 0.0).then_inc(a_free, 1)
            for kt in range(KT):
                dve.wait_ge(xT_hi_done, kt // 2 * 2 + 2)
                ins = lo_of(xT_lo[:, kt, :], aux[(kt // 2) % 4][:, (kt % 2) * SEQ:(kt % 2 + 1) * SEQ], g_norm[:, kt:kt + 1], xT_hi[:, kt, :])
                ins.then_inc(xT_lo_done, 1)
                if kt % 2 == 1:
                    dve.wait_ge(xT_lo_done, kt + 1)
                    dve.sem_inc(aux_free[(kt // 2) % 4], 1)
                if kt % 2 == 1:
                    lo(S_PROJ + kt // 2)
                if kt == 7:
                    dve.wait_ge(gains_turned, 2)
                    v.tensor_copy(gains[:, 16:44], acc_b[:, 0, 0:28]).then_inc(gains_done, 1)
                    dve.wait_ge(gains_done, 2)
                    v.memset(stat[:, 61:62], 0.0).then_inc(b_free, 1)

            def pair(i, first=False, last=False):
                for k in range(4 if first else 0, 16):
                    lo(S_PROJ + 4 + k, i, 16, 320 if last and k >= 12 else SLOT)

            pair(0, first=True)
            with dve.Fori(1, N_PAIRS - 1) as i:
                pair(i)
            pair(N_PAIRS - 1, last=True)
            for k in range(RING):
                lo(S_ZC + k)
            dve.wait_ge(slot_used, S_SMALL + RING)
            dve.wait_ge(x_rstd, 1)
            for tb in range(TB):
                for d0, s0, n in ((0, 0, 64), (64, 32, 32), (96, 0, 32), (128, 64, 16)):
                    ins = v.tensor_scalar(kr_tok[:, tb, d0:d0 + n], acc_a[:, tb, s0:s0 + n], rstd_x[:, tb:tb + 1], None, ALU.mult)
                    ins.then_inc(kr_done, 1)
            dve.wait_ge(kr_done, 8)
            dve.sem_inc(a_free, 1)
            dve.wait_ge(c_rstd, 1)
            for c in range(2):
                for tb in range(TB):
                    part_ = c_tok[:, tb, c * LORA:(c + 1) * LORA]
                    v.tensor_scalar(part_, part_, rstd_c[:, 2 * c + tb:2 * c + tb + 1], None, ALU.mult).then_inc(c_scaled, 1)

            def rope(dst, bank, done, part_sem, at):
                v.tensor_tensor(dst, bank[0:ROPE], rope_tab[0:ROPE, :], ALU.mult).then_inc(part_sem, 1)
                v.tensor_tensor(rope_tmp, bank[ROPE:P], rope_tab[ROPE:P, :], ALU.mult).then_inc(part_sem, 1)
                dve.wait_ge(part_sem, at)
                v.tensor_tensor(dst, dst, rope_tmp, ALU.add).then_inc(done, 1)

            def small_evac(a):
                bank = aux[a % 4]
                task_wait(dve, a)
                if a == A_KR:
                    dve.wait_ge(table_done, 1)
                    task_wait(dve, A_GT)
                    rope(krT[:, :], bank[:, 0:SEQ], krT_done, krT_part, 2)
                    dve.wait_ge(krT_done, 1)
                    dve.sem_inc(aux_free[a % 4], 1)
                elif a == A_GT:
                    dve.wait_ge(gateT_done, 1)
                    dve.sem_inc(aux_free[a % 4], 1)
                elif a < A_LG:
                    for n in range(2):
                        kt = 2 * (a - A_CT) + n
                        dve.wait_ge(cT_hi_done, 2 * (a - A_CT) + 2)
                        lo_of(cT_lo[:, kt, :], bank[:, n * SEQ:(n + 1) * SEQ], (g_q if kt < 4 else g_kv)[:, kt % 4:kt % 4 + 1],
                              cT_hi[:, kt, :]).then_inc(cT_lo_done, 1)
                    dve.wait_ge(cT_lo_done, kt + 1)
                    dve.sem_inc(aux_free[a % 4], 1)
                elif a < A_BAND:
                    for n in range(2):
                        h = 2 * (a - A_LG) + n
                        v.tensor_scalar(logit[:, h, :], bank[:, n * SEQ:(n + 1) * SEQ], b_gate[:, h:h + 1], None, ALU.add).then_inc(logit_done, 1)
                    dve.wait_ge(logit_done, h + 1)
                    dve.sem_inc(aux_free[a % 4], 1)
                    if a == A_BAND - 1:
                        v.scalar_tensor_tensor(out=soft, in0=logit, scalar=-1.0, in1=logit, op0=ALU.mult, op1=ALU.min).then_inc(soft_arg, 1)
                elif a < A_PW:
                    g = a - A_BAND
                    dve.wait_ge(mT_hi_done, g + 1)
                    v.tensor_tensor(y1_lo[:, 2 * g:2 * g + 2, :].rearrange("p n t -> p (n t)"), bank[:, :],
                                    y1_hi[:, 2 * g:2 * g + 2, :].rearrange("p n t -> p (n t)").bitcast(F32), ALU.subtract).then_inc(mT_lo_done, 1)
                    dve.wait_ge(mT_lo_done, g + 1)
                    dve.sem_inc(aux_free[a % 4], 1)
                elif a < A_YB:
                    g = a - A_PW
                    dve.wait_ge(z_silu, 1)
                    part_ = zb[:, :, g * 256:(g + 1) * 256]
                    v.tensor_tensor(part_, bank[:, :].rearrange("p (b n) -> p b n", b=TB), part_, ALU.mult).then_inc(yb_done, 1)
                    dve.wait_ge(yb_done, g + 1)
                    dve.sem_inc(aux_free[a % 4], 1)
                elif a < A_QK:
                    for n in range(2):
                        f = 2 * (a - A_YB) + n
                        dve.wait_ge(yb_hi_done, 2 * (a - A_YB) + 2)
                        lo_of(y0_lo[:, f, :], bank[:, n * SEQ:(n + 1) * SEQ], g_pool[:, f:f + 1], y0_hi[:, f, :]).then_inc(yb_lo_done, 1)
                    dve.wait_ge(yb_lo_done, f + 1)
                    dve.sem_inc(aux_free[a % 4], 1)

            for k, kind in enumerate(ZC_SLOTS):
                if k == 2:
                    small_evac(A_KR)
                for a in ZC_TASKS.get(k, ()):
                    if a != A_KR and a < A_QK:
                        small_evac(a)
                lo(S_ZC + k + RING, n=SLOT if k + RING >= len(ZC_SLOTS) or ZC_SLOTS[k + RING] == "z" else 512)
            v.memset(scan_keep, 1.0).then_inc(keep_set, 1)
            dve.wait_ge(keep_set, 1)
            v.memset(scan_keep.rearrange("p (c t) -> p c t", t=CHUNK)[:, :, 0:1], 0.0).then_inc(keep_set, 1)
            dve.wait_ge(soft_done, 1)
            v.scalar_tensor_tensor(out=logit, in0=logit, scalar=0.0, in1=soft, op0=ALU.min, op1=ALU.subtract).then_inc(log_a_done, 1)
            dve.wait_ge(log_a_done, 1)
            dve.wait_ge(keep_set, 2)
            task_wait(dve, A_QK - 1)
            v.tensor_tensor_scan(bcum.rearrange("p h t -> p (h t)"), scan_keep, logit.rearrange("p h t -> p (h t)"), 0.0, ALU.mult, ALU.add).then_inc(bcum_done, 1)

            def bias(n, used):
                dve.wait_ge(slot_used, used)
                dve.wait_ge(bias_landed, 16 * n + 16)
                for tb in range(TB):
                    v.scalar_tensor_tensor(out=gate[:, tb, :], in0=acc_b[:, tb, :], scalar=rstd_x[:, tb:tb + 1], in1=bias_row,
                                           op0=ALU.mult, op1=ALU.add).then_inc(bias_added, 1)
                dve.wait_ge(bias_added, 2 * n + 2)
                dve.sem_inc(b_free, 1)

            def merge(n, i, first, used):
                cols = bass.ds(i * NCOL, NCOL)
                dve.wait_ge(slot_used, used)
                dve.wait_ge(gate_done, n + 1)
                dst = merged[:, :, cols] if first else gate
                v.scalar_tensor_tensor(out=dst, in0=gate, scalar=1.0, in1=acc_a, op0=ALU.add, op1=ALU.mult).then_inc(gated, 1)
                dve.wait_ge(gated, n + 1)
                dve.sem_inc(a_free, 1)
                if first:
                    dve.sem_inc(merged_done, 1)
                else:
                    v.tensor_tensor(merged[:, :, cols], merged[:, :, cols], gate, ALU.add).then_inc(merged_done, 1)

            with dve.Fori(0, 4) as i:
                for k in range(16):
                    j = k % 2
                    if k in (4, 6):
                        j = (k - 4) // 2
                        h1 = 2 * i + j + 1
                        bank = aux[(A_B0 + 2 * j) % 4]
                        task_wait(dve, A_B0 + 2 * j, i)
                        rope(qr[j], bank[:, SEQ:2 * SEQ], qr_done, rope_part, 2 * h1)
                        dve.wait_ge(qr_done, h1)
                        dve.wait_ge(qn_done, h1)
                        dve.sem_inc(aux_free[(A_B0 + 2 * j) % 4], 1)
                    if k in (5, 7):
                        j = (k - 5) // 2
                        dve.wait_ge(kv_done, 2 * (2 * i + j + 1))
                        dve.sem_inc(aux_free[(A_B0 + 2 * j + 1) % 4], 1)
                    if k in (8, 9):
                        bank = aux[(A_B0 + 4 + j) % 4]
                        task_wait(dve, A_B0 + 4 + j, i)
                        apart(dve)
                        for tb, lo_, hi_ in ((0, 0, 128), (1, 128, 384)):
                            v.tensor_tensor_reduce(sc[j][:, lo_:hi_], bank[:, lo_:hi_], mask[:, SEQ - (hi_ - lo_):SEQ], 1.0, NEG * 2,
                                                   ALU.add, ALU.max, mx[j][:, tb:tb + 1]).then_inc(s_done, 1)
                        dve.wait_ge(s_done, 2 * (2 * i + j + 1))
                        dve.sem_inc(aux_free[(A_B0 + 4 + j) % 4], 1)
                        v.tensor_scalar(neg_m[j], mx[j], -(float(NOPE + ROPE) ** -0.5), None, ALU.mult).then_inc(m_done, 1)
                    if k in (10, 11):
                        dve.wait_ge(p_done, 2 * (2 * i + j + 1))
                        v.reciprocal(row_inv[j], row_sum[j]).then_inc(inv_done, 1)
                        dve.wait_ge(pT_done, 2 * i + j + 1)
                        dve.sem_inc(aux_free[(A_B0 + 6 + j) % 4], 1)
                    if k == 11:
                        bias(i, S_B0 + 12 + 16 * i)
                    if k in (12, 13):
                        bank = aux[(A_B0 + 8 + j) % 4]
                        task_wait(dve, A_B0 + 8 + j, i)
                        dve.wait_ge(inv_done, 2 * i + j + 1)
                        dve.wait_ge(z_silu, 2)
                        for tb in range(TB):
                            v.scalar_tensor_tensor(out=yh[:, tb, j * P:(j + 1) * P], in0=bank[:, tb * P:(tb + 1) * P], scalar=row_inv[j][:, tb:tb + 1],
                                                   in1=za[:, tb, bass.ds(i * 2 * DV + j * DV, DV)], op0=ALU.mult, op1=ALU.mult).then_inc(ya_done, 1)
                        dve.wait_ge(ya_done, 2 * (2 * i + j + 1))
                        dve.sem_inc(aux_free[(A_B0 + 8 + j) % 4], 1)
                    if k in (14, 15):
                        dve.wait_ge(ya_hi_done, 2 * i + j + 1)
                        cols = bass.ds(2 * i + j, 1)
                        v.tensor_tensor(y1_lo[:, cols, :].rearrange("p n t -> p (n t)"), aux[(A_B0 + 10 + j) % 4][:, 0:SEQ],
                                        y1_hi[:, cols, :].rearrange("p n t -> p (n t)").bitcast(F32), ALU.subtract).then_inc(ya_lo_done, 1)
                        dve.wait_ge(ya_lo_done, 2 * i + j + 1)
                        dve.sem_inc(aux_free[(A_B0 + 10 + j) % 4], 1)
                    if k == 15:
                        merge(i, i, True, S_B0 + 16 + 16 * i)
                    lo(S_B0 + k + RING, i, 16)

            task_wait(dve, A_B0 + 11, 3)
            v.memset(g_att[0:CHUNK, :, CHUNK:P], 0.0).then_inc(att_zero, 1)
            v.memset(g_att[CHUNK:P, :, 0:CHUNK], 0.0).then_inc(att_zero, 1)
            with dve.Fori(0, 4) as i:
                for k in range(12):
                    if k == 0:
                        head = bcum[:, bass.ds(i, 1), :].rearrange("p h (c t) -> p (h c) t", t=CHUNK)
                        v.tensor_scalar(b_last, head[:, :, CHUNK - 1], 1.0 / G_TAU, None, ALU.mult).then_inc(b_last_done, 1)
                        qh, kh = (m[:, bass.ds(i, 1), :].rearrange("p h t -> p (h t)") for m in (qT_all, kT_all))
                        dve.wait_ge(decays, 4 * i + 1)
                        v.scalar_tensor_tensor(out=g_q_dec, in0=qh, scalar=float(G_DK) ** -0.5, in1=g_q_dec, op0=ALU.mult, op1=ALU.mult).then_inc(g_dec_done, 1)
                        dve.wait_ge(decays, 4 * i + 2)
                        v.tensor_tensor(g_k_dec, kh, g_k_dec, ALU.mult).then_inc(g_dec_done, 1)
                        dve.wait_ge(decays, 4 * i + 3)
                        v.tensor_tensor(g_k_end, kh, g_k_end, ALU.mult).then_inc(g_dec_done, 1)
                    if k == 1:
                        bank = aux[A_B1 % 4]
                        task_wait(dve, A_B1, i)
                        for r in range(2):
                            rows_ = slice(r * CHUNK, (r + 1) * CHUNK)
                            v.tensor_copy(g_att[rows_, :, rows_], bank[rows_, 0:SEQ].rearrange("p (b i) -> p b i", b=TB)[:, :, rows_]).then_inc(att_copied, 1)
                        dve.wait_ge(att_copied, 2 * i + 2)
                        dve.sem_inc(aux_free[A_B1 % 4], 1)
                    if k == 2:
                        task_wait(dve, A_B1 + 1, i)
                        v.tensor_copy(g_k_tok, aux[(A_B1 + 1) % 4][:, 0:SEQ].rearrange("p (b d) -> p b d", b=TB)).then_inc(k_tok_done, 1)
                        dve.wait_ge(k_tok_done, i + 1)
                        dve.sem_inc(aux_free[(A_B1 + 1) % 4], 1)
                    if k == 4:
                        task_wait(dve, A_B1 + 2, i)
                        dve.wait_ge(decays, 4 * i + 4)
                        b2, b3 = aux[(A_B1 + 2) % 4], aux[(A_B1 + 3) % 4]
                        v.tensor_copy(g_state[:, 0, :], b2[:, 0:G_DV]).then_inc(state_step, 1)
                        dve.wait_ge(state_step, 3 * i + 1)
                        task_wait(dve, A_B1 + 3, i)
                        v.scalar_tensor_tensor(out=g_state[:, 1, :], in0=g_state[:, 0, :], scalar=decay[:, 1:2], in1=b3[:, 0:G_DV],
                                               op0=ALU.mult, op1=ALU.add).then_inc(state_step, 1)
                        dve.wait_ge(state_step, 3 * i + 2)
                        dve.sem_inc(aux_free[(A_B1 + 3) % 4], 1)
                        v.scalar_tensor_tensor(out=g_state[:, 2, :], in0=g_state[:, 1, :], scalar=decay[:, 2:3], in1=b2[:, G_DV:2 * G_DV],
                                               op0=ALU.mult, op1=ALU.add).then_inc(state_step, 1)
                        dve.wait_ge(state_step, 3 * i + 3)
                        dve.sem_inc(aux_free[(A_B1 + 2) % 4], 1)
                    if k == 7:
                        bias(4 + i, S_B1 + 8 + 12 * i)
                        dve.wait_ge(o_rstd, i + 1)
                        for tb in range(TB):
                            v.scalar_tensor_tensor(out=yh[:, tb, :], in0=aux[(A_B1 + 4 + tb) % 4][:, 0:G_DV], scalar=rstd_o[:, tb:tb + 1],
                                                   in1=zc[:, tb, bass.ds(i * G_DV, G_DV)], op0=ALU.mult, op1=ALU.mult).then_inc(yc_done, 1)
                        dve.wait_ge(yc_done, 2 * i + 2)
                        dve.sem_inc(aux_free[(A_B1 + 4) % 4], 1)
                        dve.sem_inc(aux_free[(A_B1 + 5) % 4], 1)
                    if k == 9:
                        for n in range(2):
                            cols = bass.ds(2 * i + n, 1)
                            dve.wait_ge(yc_hi_done, 2 * i + n + 1)
                            lo_of(y0_lo[:, cols, :].rearrange("p n t -> p (n t)"), aux[(A_B1 + 6 + n) % 4][:, 0:SEQ], g_gla[:, cols],
                                  y0_hi[:, cols, :].rearrange("p n t -> p (n t)")).then_inc(yc_lo_done, 1)
                        dve.wait_ge(yc_lo_done, 2 * i + 2)
                        dve.sem_inc(aux_free[(A_B1 + 6) % 4], 1)
                        dve.sem_inc(aux_free[(A_B1 + 7) % 4], 1)
                    if k == 11:
                        merge(4 + i, i, False, S_B1 + 12 + 12 * i)
                    lo(S_B1 + k + RING, i, 12)

            def merged_lo(n):
                dve.wait_ge(mg_hi_done, n + 1)
                lo_of(xT_lo[:, 2 * n:2 * n + 2, :].rearrange("p n t -> p (n t)"), aux[n % 4][:, :], 0.5,
                      xT_hi[:, 2 * n:2 * n + 2, :].rearrange("p n t -> p (n t)")).then_inc(mg_lo_done, 1)
                dve.wait_ge(mg_lo_done, n + 1)
                dve.sem_inc(aux_free[n % 4], 1)

            with dve.Fori(0, 3) as i:
                for k in range(12):
                    if k == 7:
                        bias(8 + i, S_B2 + 8 + 12 * i)
                    if k == 11:
                        merge(8 + i, i, False, S_B2 + 12 + 12 * i)
                    lo(S_B2 + k + RING, i, 12)
            for k in range(12):
                if k == 7:
                    bias(11, S_B2 + 36 + 8)
                if 8 <= k <= 10:
                    merged_lo(2 * (k - 8))
                    merged_lo(2 * (k - 8) + 1)
                if k == 11:
                    merge(11, 3, False, S_B2 + 48)
                lo(S_B2 + 36 + k + RING)
            for n in (6, 7):
                merged_lo(n)

            dve.wait_ge(x_again, 16)
            for k in range(32):
                if k % 8 == 7:
                    c = k // 8
                    acc_x, free = ((acc_b, b_free), (acc_a, a_free))[c % 2]
                    dve.wait_ge(slot_used, S_OUT + k + 1)
                    part_ = x_res[:, :, c * NCOL:(c + 1) * NCOL]
                    v.tensor_tensor(part_, acc_x, part_, ALU.add).then_inc(res_done, 1)
                    dve.wait_ge(res_done, c + 1)
                    dve.sem_inc(free, 1)
                if S_OUT + k + RING < S_END:
                    lo(S_OUT + k + RING)
            dve.wait_ge(f_ssq, 8)
            v.tensor_reduce(ssq_ft, ssq_f.rearrange("p (b c) -> p b c", b=TB), AX_X, ALU.add).then_inc(f_sum, 1)
            dve.wait_ge(f_rstd, 1)
            dve.wait_ge(fnorm_landed, 16)
            for q in range(4):
                tb, cols = q // 2, slice((q % 2) * WIDTH, (q % 2 + 1) * WIDTH)
                v.scalar_tensor_tensor(out=x_res[:, tb, cols], in0=x_res[:, tb, cols], scalar=rstd_f[:, tb:tb + 1], in1=fnorm_row[:, cols],
                                       op0=ALU.mult, op1=ALU.mult).then_inc(f_done, 1)


_INS = ["x", "positions", "norm_g", "w_in", "b_merge", "mla_q_norm", "mla_kv_norm", "mla_w_uq", "mla_w_ukv", "pool_w",
        "pool_scale", "gla_w_gate", "gla_b_gate", "gla_norm", "w_branch", "w_out", "final_norm"]


def kernel(**inputs):
    import concourse.bacc as _bacc
    from concourse.bass_utils import run_bass_kernel_spmd as _run

    nc = _bacc.Bacc("TRN2", target_bir_lowering=False, num_devices=1)
    arrays = {f"in_{name}_dram": np.ascontiguousarray(inputs[name]) for name in _INS}
    arrays["shape_constants_dram"] = shape_constants()
    args = [nc.dram_tensor(n, a.shape, mybir.dt.from_np(a.dtype), kind="ExternalInput").ap() for n, a in arrays.items()]
    out = nc.dram_tensor("out_dram", (1, SEQ, D), F32, kind="ExternalOutput").ap()
    trunk_kernel(nc, *args, out)
    r = _run(nc, [arrays], core_ids=[0])
    return r.results[0]["out_dram"]
```

```python
from contextlib import ExitStack

import numpy as np

import concourse.bass as bass
from concourse import mybir
from concourse.alu_op_type import AluOpType as ALU

ACT = mybir.ActivationFunctionType
F32 = mybir.dt.float32
F32R = mybir.dt.float32r
I32 = mybir.dt.int32
AX_X = mybir.AxisListType.X

P = 128
D = 2048
SEQ = 256
TB = SEQ // P
CHUNK = 64
EPS = 1e-6
HEADS, NOPE, ROPE, DV = 8, 128, 64, 128
LORA = 512
G_HEADS, G_DK, G_DV, G_RANK, G_TAU = 4, 128, 256, 16, 16.0
WINDOWS = (2, 4, 8, 16)
WIDTH = 1024
NEG = -1e30

C_Q, C_KV, C_KROPE, C_ZA = 0, LORA, 2 * LORA, 2 * LORA + ROPE
C_UB = C_ZA + WIDTH
C_ZB = C_UB + WIDTH
C_QC = C_ZB + WIDTH
C_KC = C_QC + LORA
C_VC = C_KC + LORA
C_LR = C_VC + WIDTH
C_ZC = C_LR + G_RANK
C_GATES = C_ZC + WIDTH

NCOL = 512
KT = D // P
WKT = WIDTH // P
SLOT = 1024
RING = 4
X_PARTS = (slice(0, 256), slice(256, 512), slice(512, 1024), slice(1024, 1536), slice(1536, 2048))

S_PROJ = 0
N_PAIRS = 6
S_SMALL = S_PROJ + 16 * N_PAIRS
S_ZC = S_SMALL + 4
ZC_SLOTS = ("z", "z", "z", "z", "z", "z", "z", "p", "p", "z", "z", "p", "p", "z", "z", "z", "z", "z", "z", "z")
S_B0 = S_ZC + 20
S_B1 = S_B0 + 64
S_B2 = S_B1 + 48
S_OUT = S_B2 + 48
S_END = S_OUT + 32

A_X = 0
A_SMALL = 8
A_KR = 9
A_CT = 10
A_LG = 14
A_BAND = 16
A_PW = 20
A_YB = 24
A_QK = 28
A_B0 = 32
A_B1 = A_B0 + 48
A_MT = A_B1 + 32

ZC_TASKS = {1: (9,), 2: (10, 11), 3: (12, 13), 4: (14, 15), 5: (16, 17), 6: (18, 19), 7: (20,), 8: (21,),
            11: (22,), 12: (23,), 13: (24, 25), 15: (26, 27), 16: (28, 29), 18: (30, 31)}

M_RNE = 12582912.0
TWO_PI = 2 * np.pi


def _top(x, bits):
    m, e = np.frexp(x)
    return float(np.ldexp(np.round(np.ldexp(m, bits)), int(e) - bits))


PI1 = _top(TWO_PI, 14)
PI2 = _top(TWO_PI - PI1, 14)
PI3 = float(np.float32(TWO_PI - PI1 - PI2))
TURNS = []
for _j in (3, 2, 1):
    _t = 2.0 ** (8 * _j) / TWO_PI
    _t -= np.rint(_t)
    TURNS.append((2.0 ** (8 * _j), _top(_t, 15), float(np.float32(_t - _top(_t, 15)))))

K_ID, K_MASK, K_FREQ, K_SIGN, K_SWAP, K_BAND = 0, 128, 384, 385, 386, 514
K_END = K_BAND + 4 * 384


def shape_constants():
    c = np.zeros((P, K_END), np.float32)
    c[:, K_ID:K_ID + P] = np.eye(P, dtype=np.float32)
    c[:CHUNK, K_MASK + 2 * P - CHUNK:K_MASK + 2 * P] = NEG
    half = ROPE // 2
    inv = (np.float32(1.0) / (np.float32(10000.0) ** (np.arange(0, ROPE, 2, dtype=np.float32) / np.float32(ROPE))))
    c[:, K_FREQ] = inv[np.arange(P) % half]
    rope_row = np.arange(P) % ROPE
    c[:, K_SIGN] = np.where(rope_row < half, -1.0, 1.0)
    c[np.arange(P), K_SWAP + np.arange(P) - rope_row + (rope_row + half) % ROPE] = 1.0
    t = np.arange(SEQ)
    for g, w in enumerate(WINDOWS):
        count = np.minimum(t + 1, w).astype(np.float32)
        band = ((t[:, None] <= t[None, :]) & (t[:, None] > t[None, :] - w)) / count[None, :] - np.eye(SEQ)
        c[:, K_BAND + g * 384:K_BAND + g * 384 + 256] = band[:P]
        c[:, K_BAND + g * 384 + 256:K_BAND + g * 384 + 384] = band[P:, P:]
    return c


def trunk_kernel(nc, x, positions, norm_g, w_in, b_merge, mla_q_norm, mla_kv_norm, mla_w_uq, mla_w_ukv, pool_w,
                 pool_scale, gla_w_gate, gla_b_gate, gla_norm, w_branch, w_out, final_norm, consts, out):
    x_d = x[0].rearrange("(b p) d -> p b d", p=P)
    out_d = out[0].rearrange("(b p) d -> p b d", p=P)
    w_in_d = w_in[0].rearrange("(t p) n -> p t n", p=P)
    w_uq_d = mla_w_uq[0].rearrange("(t p) (h n) -> p t h n", p=P, h=HEADS)
    w_ukv_d = mla_w_ukv[0].rearrange("(t p) (h c n) -> p t h c n", p=P, h=HEADS, c=2)
    pool_w_d = pool_w[0].rearrange("g (t p) n -> g p t n", p=P)
    w_branch_d = [w_branch[0, n].rearrange("(t p) n -> p t n", p=P) for n in range(3)]
    w_out_d = w_out[0].rearrange("(t p) n -> p t n", p=P)

    with ExitStack() as ctx:
        def sb(name, shape, dt=F32):
            return ctx.enter_context(nc.sbuf_tensor(name, shape, dt))

        def sem(name):
            return ctx.enter_context(nc.semaphore(name))

        xT_hi = sb("xT_hi", [P, KT, SEQ], F32R)
        xT_lo = sb("xT_lo", [P, KT, SEQ], F32R)
        y0_hi = sb("y0_hi", [P, WKT, SEQ], F32R)
        y0_lo = sb("y0_lo", [P, WKT, SEQ], F32R)
        y1_hi = sb("y1_hi", [P, WKT, SEQ], F32R)
        y1_lo = sb("y1_lo", [P, WKT, SEQ], F32R)
        cT_hi = sb("cT_hi", [P, 8, SEQ], F32R)
        cT_lo = sb("cT_lo", [P, 8, SEQ], F32R)
        raw = sb("raw", [P, RING, SLOT])
        w_hi = sb("w_hi", [P, RING, SLOT], F32R)
        w_lo = sb("w_lo", [P, RING, SLOT], F32R)
        xin = sb("xin", [P, TB, D])
        proj = sb("proj", [P, TB, 12 * NCOL])
        head_a = sb("head_a", [P, 1792])
        head_pT_b = sb("head_pT_b", [P, 3, P])
        yh = sb("yh", [P, TB, 2 * P])
        const = sb("const", [P, K_SWAP])
        rope_tab = sb("rope_tab", [P, 2, SEQ])
        krT_rows = sb("krT_rows", [ROPE + G_RANK, SEQ])
        gains = sb("gains", [P, 44])
        stat = sb("stat", [P, 64])

        ident = const[:, K_ID:K_ID + P]
        krT = krT_rows[0:ROPE, :]
        cos_tab, sin_tab = rope_tab[:, 0, :], rope_tab[:, 1, :]
        mask = const[:, K_MASK:K_MASK + SEQ]
        g_norm, g_q, g_kv, g_pool, g_gla, b_gate = (gains[:, a:b] for a, b in
                                                    ((0, 16), (16, 20), (20, 24), (24, 32), (32, 40), (40, 44)))
        ssq_x, rstd_x, ssq_c, rstd_c = stat[:, 0:2], stat[:, 2:4], stat[:, 4:8], stat[:, 8:12]
        minus_half = stat[:, 12:16]
        mx = [stat[:, 16:18], stat[:, 18:20]]
        neg_m = [stat[:, 20:22], stat[:, 22:24]]
        row_sum = [stat[:, 24:26], stat[:, 26:28]]
        row_inv = [stat[:, 28:30], stat[:, 30:32]]
        b_last, decay, ssq_o, rstd_o = stat[:, 32:36], stat[:, 36:40], stat[:, 40:42], stat[:, 42:44]
        ssq_f, ssq_ft, rstd_f = stat[:, 44:52], stat[:, 52:54], stat[:, 54:56]
        ms_tmp, f_mean = stat[:, 56:60], stat[:, 32:34]

        R_C, R_ZA, R_U, R_ZB, R_QK, R_V = (n * WIDTH for n in range(6))
        c_tok = proj[:, :, R_C:R_C + WIDTH]
        zc = c_tok
        za = proj[:, :, R_ZA:R_ZA + WIDTH]
        u_tok = proj[:, :, R_U:R_U + WIDTH]
        zb = proj[:, :, R_ZB:R_ZB + WIDTH]
        v_tok = proj[:, :, R_V:R_V + WIDTH]
        qT_all = proj[:, 0, R_U:R_U + WIDTH].rearrange("p (h t) -> p h t", h=G_HEADS)
        kT_all = proj[:, 1, R_U:R_U + WIDTH].rearrange("p (h t) -> p h t", h=G_HEADS)
        bcum = proj[:, 0, R_ZB:R_ZB + WIDTH].rearrange("p (h t) -> p h t", h=G_HEADS)
        head_b = proj[:, 1, R_ZB:R_ZB + WIDTH]
        gate = proj[:, 0, R_QK:R_QK + WIDTH].rearrange("p (b n) -> p b n", b=TB)
        bias_row = proj[:, 1, R_QK:R_QK + NCOL]
        s_b = proj[:, 1, R_QK + NCOL:R_QK + NCOL + 384]
        swap = proj[:, 1, R_V - P:R_V]
        swap_k = head_pT_b[0:ROPE, 0, 0:ROPE]
        x_res = proj[:, :, 0:D]
        fnorm_row = proj[:, 0, R_U:R_U + D]
        band = xin[:, 0, 0:4 * 384].rearrange("p (g t) -> p g t", g=4)
        w_gate = xin[0:G_RANK, 0, 1536:2048]
        scan_keep = xin[:, 0, 0:WIDTH]
        logit = xin[:, 1, 0:WIDTH].rearrange("p (h t) -> p h t", h=G_HEADS)
        soft = xin[:, 1, WIDTH:2 * WIDTH].rearrange("p (h t) -> p h t", h=G_HEADS)
        merged = xin
        y_out = xin
        norm_rows = proj[0:16, 1, R_QK + P:R_QK + 2 * P]
        gain_rows = proj[0:28, 1, R_QK:R_QK + P]
        gateT = xin[0:G_RANK, 1, WIDTH:WIDTH + SEQ]
        ang = [head_a[:, n * SEQ:(n + 1) * SEQ] for n in range(6)]

        qn = [head_a[:, 0:256], head_b[:, 0:256]]
        qr = [head_a[0:ROPE, 256:512], head_b[0:ROPE, 256:512]]
        kn = [head_a[:, 512:768], head_b[:, 512:768]]
        vh = [a[:, 768:1024].rearrange("p (b d) -> p b d", b=TB) for a in (head_a, head_b)]
        sc = [head_a[:, 1024:1408], s_b]
        pT = [head_a[:, 1408:1792].rearrange("p (n q) -> p n q", n=3), head_pT_b]
        q_raw, rope_tmp = yh[:, 0, :], yh[:, 1, :]
        ones = head_a[:, 6 * SEQ:6 * SEQ + ROPE + G_RANK]
        rstd_diag = yh[:, 0, :].rearrange("p (b t) -> p b t", b=TB)
        rstd_row = krT_rows[:, :]
        kr_raw = yh[0:ROPE, 1, :]

        g_state = proj[:, 0, R_ZA:R_ZA + 768].rearrange("p (n d) -> p n d", n=3)
        g_q_dec = proj[:, 0, R_ZA + 768:R_ZA + 1024]
        g_v = proj[:, 1, R_ZA:R_ZA + 512].rearrange("p (b d) -> p b d", b=TB)
        g_k_dec = proj[:, 1, R_ZA + 512:R_ZA + 768]
        g_k_end = proj[:, 1, R_ZA + 768:R_ZA + 1024]
        g_k_tok = head_a[:, 0:256].rearrange("p (b d) -> p b d", b=TB)
        g_att = head_a[:, 512:768].rearrange("p (b i) -> p b i", b=TB)
        g_junk = head_a[:, 1024:1280]

        acc = ctx.enter_context(nc.psum_tensor("acc", [P, 4, NCOL], F32))
        acc_a, acc_b = acc[:, 0:2, :], acc[:, 2:4, :]
        aux = [ctx.enter_context(nc.psum_tensor(f"aux{k}", [P, NCOL], F32)) for k in range(4)]

        x_landed = [sem(f"x_landed{k}") for k in range(len(X_PARTS))]
        rest_landed = sem("rest_landed")
        const_landed, gains_landed, pos_landed = sem("const_landed"), sem("gains_landed"), sem("pos_landed")
        norm_landed = sem("norm_landed")
        gains_turned, gains_done = sem("gains_turned"), sem("gains_done")
        band_landed, bias_landed, x_again, fnorm_landed = sem("band_landed"), sem("bias_landed"), sem("x_again"), sem("fnorm_landed")
        slot_landed = [sem(f"slot_landed{k}") for k in range(RING)]
        second_landed = [sem(f"second_landed{k}") for k in range(4)]
        hi_ready, lo_ready, slot_used = sem("hi_ready"), sem("lo_ready"), sem("slot_used")
        aux_ready = sem("aux_ready")
        waited = sem("waited")
        aux_free = [sem(f"aux_free{k}") for k in range(4)]
        a_free, b_free = sem("a_free"), sem("b_free")
        x_ssq, x_ms, x_rstd = sem("x_ssq"), sem("x_ms"), sem("x_rstd")
        xT_hi_done, xT_lo_done = sem("xT_hi_done"), sem("xT_lo_done")
        pool_const, angle_step, angle_done, table_done = sem("pool_const"), sem("angle_step"), sem("angle_done"), sem("table_done")
        diag_done, row_done, kr_done, krT_part, krT_done, gateT_done = (sem("diag_done"), sem("row_done"), sem("kr_done"),
                                                                        sem("krT_part"), sem("krT_done"), sem("gateT_done"))
        swap_landed, q_raw_done, swapped = sem("swap_landed"), sem("q_raw_done"), sem("swapped")
        c_ssq, c_ms, c_rstd, c_scaled = sem("c_ssq"), sem("c_ms"), sem("c_rstd"), sem("c_scaled")
        cT_hi_done, cT_lo_done = sem("cT_hi_done"), sem("cT_lo_done")
        logit_done, soft_arg, soft_exp, soft_done = sem("logit_done"), sem("soft_arg"), sem("soft_exp"), sem("soft_done")
        keep_set, log_a_done, bcum_done = sem("keep_set"), sem("log_a_done"), sem("bcum_done")
        mT_hi_done, mT_lo_done = sem("mT_hi_done"), sem("mT_lo_done")
        z_silu, yb_done, yb_hi_done, yb_lo_done = sem("z_silu"), sem("yb_done"), sem("yb_hi_done"), sem("yb_lo_done")
        rope_part, qr_done, qn_done, kv_done = sem("rope_part"), sem("qr_done"), sem("qn_done"), sem("kv_done")
        s_done, m_done, p_done, inv_done = sem("s_done"), sem("m_done"), sem("p_done"), sem("inv_done")
        pT_done, ya_done, ya_hi_done, ya_lo_done = sem("pT_done"), sem("ya_done"), sem("ya_hi_done"), sem("ya_lo_done")
        bias_added, gate_done, gated, merged_done = sem("bias_added"), sem("gate_done"), sem("gated"), sem("merged_done")
        b_last_done, decays, g_v_done, g_dec_done = sem("b_last_done"), sem("decays"), sem("g_v_done"), sem("g_dec_done")
        att_copied, att_done, k_tok_done, state_step = sem("att_copied"), sem("att_done"), sem("k_tok_done"), sem("state_step")
        att_zero = sem("att_zero")
        o_ssq, o_ms, o_rstd, yc_done, yc_hi_done, yc_lo_done = sem("o_ssq"), sem("o_ms"), sem("o_rstd"), sem("yc_done"), sem("yc_hi_done"), sem("yc_lo_done")
        last_done, y_done, f_done_act = sem("last_done"), sem("y_done"), sem("f_done_act")
        mg_hi_done, mg_lo_done = sem("mg_hi_done"), sem("mg_lo_done")
        res_done, f_ssq, f_sum, f_ms, f_rstd, f_done, stored = (sem("res_done"), sem("f_ssq"), sem("f_sum"), sem("f_ms"), sem("f_rstd"), sem("f_done"),
                                                        sem("stored"))

        def landed(s, i=0, per=0):
            return 16 + 16 * (s // RING) + (16 if s + (i * per if isinstance(i, int) else 0) >= S_SMALL else 0) + (per // RING) * 16 * i

        def apart(eng):
            eng.sem_inc(waited, 1)

        def aux_wait(eng, a, i=0, per=0):
            if a >= 4:
                eng.wait_ge(aux_free[a % 4], a // 4 + (per // 4) * i)

        own_slot = {A_SMALL: S_SMALL + 3}
        own_slot |= {A_PW + n: S_ZC + k for n, k in enumerate([k for k, kind in enumerate(ZC_SLOTS) if kind == "p"])}
        head_slot = {A_B0 + n: S_B0 + 4 + n for n in range(4)}

        def counted(a):
            return a - sum(b < a for b in (*own_slot, *head_slot)) - (12 if a >= A_B1 else 0)

        def task_wait(eng, a, i=0):
            if a in own_slot:
                eng.wait_ge(slot_used, own_slot[a] + 1)
            elif a in head_slot:
                eng.wait_ge(slot_used, head_slot[a] + 1 + 16 * i)
            else:
                eng.wait_ge(aux_ready, counted(a) + 1 + 8 * i)

        block = ctx.enter_context(nc.Block())

        @block.sync
        def _(sp):
            def load(s, dst_n, src, i=0, per=0, shape=None):
                if s >= RING:
                    sp.wait_ge(lo_ready, s - RING + 1 + per * i)
                    apart(sp)
                dst = raw[:, s % RING, 0:dst_n].rearrange("p (t n) -> p t n", t=shape)
                return sp.dma_start(dst, src)

            def load_chunk(s, src, col, k, i=0, per=0):
                load(s, SLOT, src[:, 2 * k:2 * k + 2, bass.ds(col, NCOL)], i, per, 2).then_inc(slot_landed[s % RING], 16)

            for c, col in enumerate((C_Q, C_KV)):
                for k in range(8):
                    if c == 0 and k < 4:
                        for n in (0, 1, 2) if k == 0 else (k + 2,) if k < 3 else ():
                            cols = X_PARTS[n]
                            sp.dma_start(xin[:, :, cols], x_d[:, :, cols]).then_inc(x_landed[n], 16)
                    load_chunk(S_PROJ + 8 * c + k, w_in_d, col, k)
                    if c == 0 and k == 3:
                        sp.dma_start(const[:, P:], consts[:, P:K_SWAP]).then_inc(rest_landed, 16)
                        sp.dma_start(ang[0].bitcast(I32), positions[0].partition_broadcast(P)).then_inc(pos_landed, 16)
                        row = 0
                        for src in (mla_q_norm, mla_kv_norm, pool_scale, gla_norm, gla_b_gate):
                            n = src.shape[1] // P
                            sp.dma_start(gain_rows[row:row + n, :], src[0].rearrange("(t p) -> t p", p=P)).then_inc(gains_landed, 16)
                            row += n
                        sp.dma_start(swap_k, consts[0:ROPE, K_SWAP:K_SWAP + ROPE]).then_inc(swap_landed, 16)
            task_wait(sp, A_X + 7)
            sp.wait_ge(x_ssq, 2)
            sp.dma_start(band, consts[:, K_BAND:K_END].rearrange("p (g t) -> p g t", g=4)).then_inc(band_landed, 16)
            sp.dma_start(w_gate, gla_w_gate[0]).then_inc(band_landed, 16)
            with sp.Fori(0, N_PAIRS - 1) as i:
                for c in range(2):
                    for k in range(8):
                        load_chunk(S_PROJ + 16 + 8 * c + k, w_in_d, C_ZA + c * NCOL + i * WIDTH, k, i, 16)
            for k in range(RING):
                s = S_SMALL + k
                sp.wait_ge(lo_ready, s - RING + 1)
                dst = raw[:, s % RING, 0:4 * 80].rearrange("p (t n) -> p t n", t=4)
                sp.dma_start(dst[:, :, 0:ROPE], w_in_d[:, 4 * k:4 * k + 4, C_KROPE:C_KROPE + ROPE]).then_inc(slot_landed[s % RING], 16)
                sp.dma_start(dst[:, :, ROPE:80], w_in_d[:, 4 * k:4 * k + 4, C_LR:C_LR + G_RANK]).then_inc(slot_landed[s % RING], 16)
            z = p = 0
            for k, kind in enumerate(ZC_SLOTS):
                if kind == "z":
                    load_chunk(S_ZC + k, w_in_d, C_ZC + NCOL * (z // 8), z % 8)
                    z += 1
                else:
                    load(S_ZC + k, 2 * 256, pool_w_d[p], shape=2).then_inc(slot_landed[(S_ZC + k) % RING], 16)
                    p += 1

            def load_turn(s0, per, n, gate_no, i, heads):
                gcol = C_GATES + n * D + i * NCOL
                for k in range(4):
                    load_chunk(s0 + k, w_in_d, gcol, k, i, per)
                task_wait(sp, A_QK + 3)
                sp.wait_ge(b_free, gate_no + 8 + i)
                apart(sp)
                sp.dma_start(bias_row, b_merge[0, n, bass.ds(i * NCOL, NCOL)].partition_broadcast(P)).then_inc(bias_landed, 16)
                k = 4
                if heads:
                    for j in range(4):
                        s = s0 + 4 + j
                        width = ROPE if j == 0 else P
                        sp.wait_ge(lo_ready, s - RING + 1 + per * i)
                        apart(sp)
                        dst = raw[:, s % RING, 0:8 * width].rearrange("p (t h n) -> p t h n", t=4, h=2)
                        for m, landed_ in enumerate((slot_landed[s % RING], second_landed[j])):
                            h = 2 * i + m
                            src = (w_uq_d[:, :, h, NOPE:], w_uq_d[:, :, h, 0:NOPE], w_ukv_d[:, :, h, 0, :], w_ukv_d[:, :, h, 1, :])[j]
                            sp.dma_start(dst[:, :, m, :], src).then_inc(landed_, 16)
                    k = 8
                for g in range(4, 8):
                    load_chunk(s0 + k, w_in_d, gcol, g, i, per)
                    k += 1
                for g in range(4):
                    load_chunk(s0 + k, w_branch_d[n], i * NCOL, g, i, per)
                    k += 1

            with sp.Fori(0, 4) as i:
                load_turn(S_B0, 16, 1, 0, i, True)
            with sp.Fori(0, 4) as i:
                load_turn(S_B1, 12, 0, 4, i, False)
            with sp.Fori(0, 4) as i:
                load_turn(S_B2, 12, 2, 8, i, False)
            sp.wait_ge(slot_used, S_B2 + 12)
            sp.dma_start(x_res, x_d).then_inc(x_again, 16)
            sp.dma_start(fnorm_row, final_norm.partition_broadcast(P)).then_inc(fnorm_landed, 16)
            with sp.Fori(0, 2) as i:
                for c in range(2):
                    for k in range(8):
                        load_chunk(S_OUT + 8 * c + k, w_out_d, c * NCOL + i * WIDTH, k, i, 16)
            for tb in range(TB):
                for cols, done in ((slice(0, WIDTH), f_done), (slice(WIDTH, D), f_done_act)):
                    sp.wait_ge(done, tb + 1)
                    sp.dma_start(out_d[:, tb, cols], y_out[:, tb, cols]).then_inc(stored, 16)
            sp.wait_ge(stored, 64)

        @block.gpsimd
        def _(pool):
            nc.gpsimd.memset(minus_half, -0.5).then_inc(pool_const, 1)
            pool.wait_ge(pool_const, 1)

            def inv_root(out_, ssq, n, of, ready, at, mid, done, at_mid):
                pool.wait_ge(ready, at)
                apart(pool)
                nc.gpsimd.tensor_scalar(ms_tmp[:, 0:n], ssq, 1.0 / of, EPS, ALU.mult, ALU.add).then_inc(mid, 1)
                pool.wait_ge(mid, at_mid)
                nc.gpsimd.tensor_tensor(out_, ms_tmp[:, 0:n], minus_half[:, 0:n], ALU.pow).then_inc(done, 1)

            inv_root(rstd_x, ssq_x, 2, D, x_ssq, 2, x_ms, x_rstd, 1)

            count = [0]

            def step(ins):
                count[0] += 1
                ins.then_inc(angle_step, 1)
                pool.wait_ge(angle_step, count[0])

            def ts(o, i0, s0, s1, op0, op1=None):
                if op1 is None:
                    step(nc.gpsimd.tensor_scalar(o, i0, s0, None, op0))
                else:
                    step(nc.gpsimd.tensor_scalar(o, i0, s0, s1, op0, op1))

            def tt(o, i0, i1, op):
                step(nc.gpsimd.tensor_tensor(o, i0, i1, op))

            pos_i, a, part, t, r, turns = ang[0].bitcast(I32), ang[1], ang[2], ang[3], ang[4], ang[5]
            pool.wait_ge(pos_landed, 16)
            pool.wait_ge(rest_landed, 16)
            step(nc.gpsimd.tensor_copy(a, pos_i))
            ts(a, a, const[:, K_FREQ:K_FREQ + 1], None, ALU.mult)
            step(nc.gpsimd.memset(turns, 0.0))
            for scale, top, low in TURNS:
                ts(part, a, 1.0 / scale, M_RNE, ALU.mult, ALU.add)
                ts(part, part, M_RNE, None, ALU.subtract)
                ts(t, part, -scale, None, ALU.mult)
                tt(a, a, t, ALU.add)
                ts(t, part, top, None, ALU.mult)
                ts(r, t, M_RNE, None, ALU.add)
                ts(r, r, M_RNE, None, ALU.subtract)
                tt(t, t, r, ALU.subtract)
                tt(turns, turns, t, ALU.add)
                ts(t, part, low, None, ALU.mult)
                tt(turns, turns, t, ALU.add)

            def reduce(v):
                ts(part, v, 1.0 / TWO_PI, M_RNE, ALU.mult, ALU.add)
                ts(part, part, M_RNE, None, ALU.subtract)
                for p_i in (PI1, PI2, PI3):
                    ts(t, part, -p_i, None, ALU.mult)
                    tt(v, v, t, ALU.add)

            reduce(a)
            ts(r, turns, M_RNE, None, ALU.add)
            ts(r, r, M_RNE, None, ALU.subtract)
            tt(turns, turns, r, ALU.subtract)
            ts(t, turns, float(np.float32(TWO_PI)), None, ALU.mult)
            tt(a, a, t, ALU.add)
            reduce(a)
            lim = 3.1415925
            ts(a, a, lim, -lim, ALU.min, ALU.max)
            ts(t, a, 0.0, 2.0, ALU.max, ALU.mult)
            tt(t, t, a, ALU.subtract)
            ts(cos_tab, t, -1.0, float(np.float32(np.pi / 2)), ALU.mult, ALU.add)
            nc.gpsimd.tensor_scalar(sin_tab, a, const[:, K_SIGN:K_SIGN + 1], None, ALU.mult).then_inc(angle_done, 1)

            pool.wait_ge(angle_done, 1)
            inv_root(rstd_c, ssq_c, 4, LORA, c_ssq, 4, c_ms, c_rstd, 1)

            with pool.Fori(0, 4) as i:
                pool.wait_ge(att_copied, 2 * i + 2)
                apart(pool)
                nc.gpsimd.affine_select(out=g_att, in_=g_att, compare_op=ALU.is_ge, fill=0.0, base=0,
                                        pattern=[[0, TB], [1, P]], channel_multiplier=-1).then_inc(att_done, 1)
                inv_root(rstd_o, ssq_o, 2, G_DV, o_ssq, 2 * i + 2, o_ms, o_rstd, i + 1)
            for tb in range(TB):
                pool.wait_ge(f_ms, tb + 1)
                nc.gpsimd.tensor_tensor(rstd_f[:, tb:tb + 1], f_mean[:, tb:tb + 1], minus_half[:, 0:1], ALU.pow).then_inc(f_rstd, 1)

        @block.tensor
        def _(pe):
            mm = nc.tensor.matmul

            def mm3(o, s_hi, s_lo, m_hi, m_lo, start, stop):
                mm(o, s_hi, m_hi, start=start, stop=False)
                mm(o, s_hi, m_lo, start=False, stop=False)
                return mm(o, s_lo, m_hi, start=False, stop=stop)

            def rows(s_hi, s_lo, acc_x, s, kts, n_kt, i=0, per=0, width=NCOL):
                pe.wait_ge(lo_ready, s + 1 + per * i)
                k = s % RING
                for n, kt in enumerate(kts):
                    for tb in range(TB):
                        cols, tok = slice(n * width, (n + 1) * width), slice(tb * P, (tb + 1) * P)
                        last = mm3(acc_x[:, tb, 0:width], s_hi[:, kt, tok], s_lo[:, kt, tok],
                                   w_hi[:, k, cols], w_lo[:, k, cols], kt == 0, kt == n_kt - 1)
                return last

            def chunk_slot(s, k, acc_x, free, free_at, i=0, per=0, s_hi=xT_hi, s_lo=xT_lo, n_slots=8):
                if k == 0:
                    pe.wait_ge(free, free_at)
                rows(s_hi, s_lo, acc_x, s, (2 * k, 2 * k + 1), 2 * n_slots, i, per).then_inc(slot_used, 1)

            def transposes(a, pairs, i=0, per=0):
                aux_wait(pe, a, i, per)
                for o, src in pairs:
                    last = nc.tensor.transpose(o, src, ident[0:src.shape[0], 0:src.shape[0]])
                last.then_inc(aux_ready, 1)

            def first_slot(k):
                pe.wait_ge(xT_lo_done, 2 * k + 2)
                chunk_slot(S_PROJ + k, k, acc_a, a_free, 1)

            pe.wait_ge(const_landed, 16)
            pe.wait_ge(norm_landed, 16)
            nc.tensor.transpose(acc_a[:, 0, 0:16], norm_rows, ident[0:16, 0:16]).then_inc(gains_turned, 1)
            for a in range(8):
                pe.wait_ge(x_landed[a if a < 2 else a // 2 + 1], 16)
                if a >= 4:
                    first_slot(a - 4)
                transposes(A_X + a, [(aux[a % 4][:, (2 * n + tb) * P:(2 * n + tb + 1) * P],
                                      xin[:, tb, (2 * a + n) * P:(2 * a + n + 1) * P]) for n in range(2) for tb in range(TB)])
            for k in range(4, 8):
                first_slot(k)
                if k == 5:
                    pe.wait_ge(gains_landed, 80)
                    nc.tensor.transpose(acc_b[:, 0, 0:28], gain_rows, ident[0:28, 0:28]).then_inc(gains_turned, 1)
            for k in range(8):
                chunk_slot(S_PROJ + 8 + k, k, acc_b, b_free, 1)
            with pe.Fori(0, N_PAIRS - 1) as i:
                for k in range(8):
                    chunk_slot(S_PROJ + 16 + k, k, acc_a, a_free, i + 2, i, 16)
                for k in range(8):
                    chunk_slot(S_PROJ + 24 + k, k, acc_b, b_free, i + 2, i, 16)
            n_small = ROPE + G_RANK
            bank = aux[A_SMALL % 4]
            aux_wait(pe, A_SMALL)
            pe.wait_ge(diag_done, 3)
            for tb in range(TB):
                mm(bank[0:n_small, SEQ + tb * P:SEQ + (tb + 1) * P], ones, rstd_diag[:, tb, :], start=True, stop=True)
            for k in range(RING):
                s = S_SMALL + k
                pe.wait_ge(lo_ready, s + 1)
                for n in range(4):
                    cols, kt = slice(n * n_small, (n + 1) * n_small), 4 * k + n
                    last = mm3(bank[0:n_small, 0:SEQ], w_hi[:, s % RING, cols], w_lo[:, s % RING, cols],
                               xT_hi[:, kt, :], xT_lo[:, kt, :], kt == 0, kt == KT - 1)
                last.then_inc(slot_used, 1)

            def small_task(a):
                bank = aux[a % 4]
                if a == A_KR:
                    aux_wait(pe, a)
                    pe.wait_ge(kr_done, 1)
                    pe.wait_ge(swap_landed, 16)
                    mm(bank[0:ROPE, 0:SEQ], swap_k, kr_raw, start=True, stop=True).then_inc(aux_ready, 1)
                elif a < A_LG:
                    n0 = 2 * (a - A_CT)
                    pe.wait_ge(c_scaled, 4)
                    transposes(a, [(bank[:, (2 * n + tb) * P:(2 * n + tb + 1) * P], c_tok[:, tb, (n0 + n) * P:(n0 + n + 1) * P])
                                   for n in range(2) for tb in range(TB)])
                elif a < A_BAND:
                    aux_wait(pe, a)
                    pe.wait_ge(gateT_done, 1)
                    pe.wait_ge(band_landed, 32)
                    for n in range(2):
                        h = 2 * (a - A_LG) + n
                        last = mm(bank[:, n * SEQ:(n + 1) * SEQ], w_gate[:, h * G_DK:(h + 1) * G_DK], gateT, start=True, stop=True)
                    last.then_inc(aux_ready, 1)
                elif a < A_PW:
                    g = a - A_BAND
                    aux_wait(pe, a)
                    for n in range(2):
                        col = g * 256 + n * P
                        mm(bank[:, n * SEQ:(n + 1) * SEQ], u_tok[:, 0, col:col + P], band[:, g, 0:SEQ], start=True, stop=False)
                        last = mm(bank[:, n * SEQ + P:(n + 1) * SEQ], u_tok[:, 1, col:col + P], band[:, g, SEQ:SEQ + P], start=False, stop=True)
                    last.then_inc(aux_ready, 1)
                elif a < A_YB:
                    g = a - A_PW
                    s = S_ZC + [k for k, kind in enumerate(ZC_SLOTS) if kind == "p"][g]
                    aux_wait(pe, a)
                    pe.wait_ge(mT_lo_done, g + 1)
                    pe.wait_ge(lo_ready, s + 1)
                    for tb in range(TB):
                        for kt in range(2):
                            tok, cols = slice(tb * P, (tb + 1) * P), slice(kt * 256, (kt + 1) * 256)
                            last = mm3(bank[:, tb * 256:(tb + 1) * 256], y1_hi[:, 2 * g + kt, tok], y1_lo[:, 2 * g + kt, tok],
                                       w_hi[:, s % RING, cols], w_lo[:, s % RING, cols], kt == 0, kt == 1)
                    last.then_inc(slot_used, 1)
                elif a < A_QK:
                    g = a - A_YB
                    pe.wait_ge(yb_done, g + 1)
                    transposes(a, [(bank[:, (2 * n + tb) * P:(2 * n + tb + 1) * P], zb[:, tb, (2 * g + n) * P:(2 * g + n + 1) * P])
                                   for n in range(2) for tb in range(TB)])
                else:
                    n0 = 2 * (a - A_QK)
                    transposes(a, [(bank[:, (2 * n + tb) * P:(2 * n + tb + 1) * P], proj[:, tb, R_QK + (n0 + n) * P:R_QK + (n0 + n + 1) * P])
                                   for n in range(2) for tb in range(TB)])

            z = 0
            for k, kind in enumerate(ZC_SLOTS):
                if kind == "z":
                    acc_x, free, at = ((acc_b, b_free, 7), (acc_a, a_free, 7))[z // 8]
                    chunk_slot(S_ZC + k, z % 8, acc_x, free, at)
                    z += 1
                for a in ZC_TASKS.get(k, ()):
                    small_task(a)

            def gate_slot(s, k, n_gate, i, per):
                chunk_slot(s, k, acc_b, b_free, n_gate + 8 + i, i, per)

            def branch_slot(s, k, n_gate, i, per, y_hi, y_lo):
                chunk_slot(s, k, acc_a, a_free, n_gate + 8 + i, i, per, y_hi, y_lo, 4)

            with pe.Fori(0, 4) as i:
                def at(k):
                    return aux[(A_B0 + k) % 4], A_B0 + k
                for k in range(4):
                    gate_slot(S_B0 + k, k, 0, i, 16)
                pe.wait_ge(yb_lo_done, 8)
                for j in range(4):
                    s, (bank, a) = S_B0 + 4 + j, at(j)
                    pe.wait_ge(lo_ready, s + 1 + 16 * i)
                    if j == 0:
                        pe.wait_ge(cT_lo_done, 8)
                    aux_wait(pe, a, i, 12)
                    w, c0, n_w = s % RING, 4 * (j // 2), P if j == 0 else 2 * P
                    for n in range(1 if j == 0 else 2):
                        for kt in range(4):
                            o = bank[:, n * SEQ:(n + 1) * SEQ]
                            if j < 3:
                                cols = slice(kt * n_w + n * P, kt * n_w + (n + 1) * P)
                                last = mm3(o, w_hi[:, w, cols], w_lo[:, w, cols], cT_hi[:, c0 + kt, :], cT_lo[:, c0 + kt, :], kt == 0, kt == 3)
                            else:
                                cols, tok = slice(kt * n_w, (kt + 1) * n_w), slice(n * P, (n + 1) * P)
                                last = mm3(o, cT_hi[:, c0 + kt, tok], cT_lo[:, c0 + kt, tok], w_hi[:, w, cols], w_lo[:, w, cols], kt == 0, kt == 3)
                    last.then_inc(slot_used, 1)
                    if j == 1:
                        pe.wait_ge(swap_landed, 32)
                        pe.wait_ge(q_raw_done, i + 1)
                        mm(at(0)[0][:, SEQ:2 * SEQ], swap, q_raw, start=True, stop=True).then_inc(swapped, 1)

                def head_scores(j):
                    bank, a = at(4 + j)
                    aux_wait(pe, a, i, 12)
                    pe.wait_ge(krT_done, 1)
                    pe.wait_ge(qr_done, 2 * i + j + 1)
                    pe.wait_ge(qn_done, 2 * i + j + 1)
                    pe.wait_ge(kv_done, 4 * i + j + 1)
                    for tb, lo, hi in ((0, 0, 128), (1, 128, 384)):
                        tok = slice(tb * P, (tb + 1) * P)
                        mm(bank[:, lo:hi], qn[j][:, tok], kn[j][:, 0:hi - lo], start=True, stop=False)
                        last = mm(bank[:, lo:hi], qr[j][:, tok], krT[:, 0:hi - lo], start=False, stop=True)
                    last.then_inc(aux_ready, 1)

                def head_p(j):
                    bank, a = at(6 + j)
                    pe.wait_ge(p_done, 2 * (2 * i + j + 1))
                    transposes(a, [(bank[:, n * P:(n + 1) * P], sc[j][:, n * P:(n + 1) * P]) for n in range(3)], i, 12)

                def head_o(j):
                    bank, a = at(8 + j)
                    aux_wait(pe, a, i, 12)
                    pe.wait_ge(pT_done, 2 * i + j + 1)
                    pe.wait_ge(kv_done, 4 * i + 3 + j)
                    mm(bank[:, 0:P], pT[j][:, 0, :], vh[j][:, 0, :], start=True, stop=True)
                    mm(bank[:, P:2 * P], pT[j][:, 1, :], vh[j][:, 0, :], start=True, stop=False)
                    mm(bank[:, P:2 * P], pT[j][:, 2, :], vh[j][:, 1, :], start=False, stop=True).then_inc(aux_ready, 1)

                def head_y(j):
                    bank, a = at(10 + j)
                    pe.wait_ge(ya_done, 2 * (2 * i + j + 1))
                    transposes(a, [(bank[:, tb * P:(tb + 1) * P], yh[:, tb, j * P:(j + 1) * P]) for tb in range(TB)], i, 12)

                for k, work in enumerate((head_scores, head_p)):
                    for j in range(2):
                        gate_slot(S_B0 + 8 + 2 * k + j, 4 + 2 * k + j, 0, i, 16)
                        work(j)
                for k, work in enumerate((head_o, head_y)):
                    for j in range(2):
                        branch_slot(S_B0 + 12 + 2 * k + j, 2 * k + j, 0, i, 16, y0_hi, y0_lo)
                        work(j)

            with pe.Fori(0, 4) as i:
                def g_bank(k):
                    aux_wait(pe, A_B1 + k, i, 8)
                    return aux[(A_B1 + k) % 4]

                for k in range(12):
                    if k < 8:
                        gate_slot(S_B1 + k, k, 4, i, 12)
                    else:
                        if k == 8:
                            pe.wait_ge(ya_lo_done, HEADS)
                        branch_slot(S_B1 + k, k - 8, 4, i, 12, y1_hi, y1_lo)
                    if k == 2:
                        bank = g_bank(0)
                        pe.wait_ge(g_dec_done, 3 * i + 2)
                        for tb in range(TB):
                            tok = slice(tb * P, (tb + 1) * P)
                            last = mm(bank[:, tok], g_k_dec[:, tok], g_q_dec[:, tok], start=True, stop=True)
                        last.then_inc(aux_ready, 1)
                    if k == 3:
                        pe.wait_ge(g_dec_done, 3 * i + 3)
                        transposes(A_B1 + 1, [(aux[(A_B1 + 1) % 4][:, tb * P:(tb + 1) * P], g_k_end[:, tb * P:(tb + 1) * P]) for tb in range(TB)], i, 8)
                    if k == 4:
                        pe.wait_ge(k_tok_done, i + 1)
                        pe.wait_ge(g_v_done, i + 1)
                        for t_, chunks in ((2, (0, 2)), (3, (1,))):
                            bank = g_bank(t_)
                            for n, c in enumerate(chunks):
                                r0 = CHUNK * (c % 2)
                                last = mm(bank[:, n * G_DV:(n + 1) * G_DV], g_k_tok[r0:r0 + CHUNK, c // 2, :],
                                          g_v[r0:r0 + CHUNK, c // 2, :], start=True, stop=True)
                            last.then_inc(aux_ready, 1)
                    if k == 6:
                        pe.wait_ge(att_done, i + 1)
                        pe.wait_ge(state_step, 3 * i + 3)
                        for tb in range(TB):
                            bank = g_bank(4 + tb)
                            last = mm(bank[:, 0:G_DV], g_att[:, tb, :], g_v[:, tb, :], start=True, stop=True)
                            for c in (2 * tb, 2 * tb + 1):
                                if c:
                                    r0 = CHUNK * (c % 2)
                                    last = mm(bank[r0:r0 + CHUNK, 0:G_DV], g_q_dec[:, c * CHUNK:(c + 1) * CHUNK],
                                              g_state[:, c - 1, :], start=False, stop=True, skip_group_check=True)
                            last.then_inc(aux_ready, 1)
                    if k == 9:
                        pe.wait_ge(yc_done, 2 * i + 2)
                        for n in range(2):
                            a = A_B1 + 6 + n
                            transposes(a, [(aux[a % 4][:, tb * P:(tb + 1) * P], yh[:, tb, n * P:(n + 1) * P]) for tb in range(TB)], i, 8)

            def merge_turn(k, i):
                if k < 8:
                    gate_slot(S_B2 + k, k, 8, i, 12)
                else:
                    if k == 8:
                        pe.wait_ge(yc_lo_done, 8)
                    branch_slot(S_B2 + k, k - 8, 8, i, 12, y0_hi, y0_lo)

            def merged_task(n, after):
                pe.wait_ge(merged_done, after)
                transposes(A_MT + n, [(aux[n % 4][:, (2 * m + tb) * P:(2 * m + tb + 1) * P],
                                       merged[:, tb, (2 * n + m) * P:(2 * n + m + 1) * P]) for m in range(2) for tb in range(TB)])

            with pe.Fori(0, 3) as i:
                for k in range(12):
                    merge_turn(k, i)
            for k in range(12):
                merge_turn(k, 3)
                if 8 <= k <= 10:
                    for n in range(2 * (k - 8), 2 * (k - 8) + 2):
                        merged_task(n, 11)

            for c in range(4):
                acc_x, free = ((acc_b, b_free), (acc_a, a_free))[c % 2]
                for k in range(8):
                    s = S_OUT + 8 * c + k
                    if c == 0:
                        pe.wait_ge(mg_lo_done, k + 1)
                    if k == 0:
                        pe.wait_ge(free, 20 + c // 2)
                    if s < S_END - 2:
                        rows(xT_hi, xT_lo, acc_x, s, (2 * k, 2 * k + 1), KT).then_inc(slot_used, 1)
                    elif s == S_END - 1:
                        pe.wait_ge(lo_ready, s + 1)
                        for tb in range(TB):
                            for kt in range(2 * k - 2, 2 * k + 2):
                                w, tok = (s - 1 + (kt - 2 * k + 2) // 2) % RING, slice(tb * P, (tb + 1) * P)
                                cols = slice(kt % 2 * NCOL, (kt % 2 + 1) * NCOL)
                                last = mm3(acc_x[:, tb, :], xT_hi[:, kt, tok], xT_lo[:, kt, tok],
                                           w_hi[:, w, cols], w_lo[:, w, cols], False, kt == KT - 1)
                            last.then_inc(last_done, 1)
                    if c == 0 and k in (3, 4):
                        merged_task(k + 3, 12)

        @block.scalar
        def _(act):
            fn = nc.scalar.activation

            def hi(s, i=0, per=0, n=SLOT):
                k = s % RING
                act.wait_ge(slot_landed[k], landed(s, i, per))
                if s >= RING:
                    act.wait_ge(slot_used, s - RING + 1 + per * i)
                fn(w_hi[:, k, 0:n], raw[:, k, 0:n], ACT.Copy).then_inc(hi_ready, 1)

            act.dma_start(ident, consts[:, K_ID:K_ID + P]).then_inc(const_landed, 16)
            act.dma_start(norm_rows, norm_g[0].rearrange("(t p) -> t p", p=P)).then_inc(norm_landed, 16)
            act.wait_ge(pool_const, 1)
            fn(stat[:, 63:64], minus_half[:, 0:1], ACT.Copy)
            act.wait_ge(gains_done, 1)
            for kt in range(KT):
                task_wait(act, A_X + kt // 2)
                fn(xT_hi[:, kt, :], aux[(kt // 2) % 4][:, (kt % 2) * SEQ:(kt % 2 + 1) * SEQ], ACT.Copy, scale=g_norm[:, kt:kt + 1]).then_inc(xT_hi_done, 1)
                if kt % 2 == 1:
                    hi(S_PROJ + kt // 2)

            def pair(i, first=False, last=False):
                for k in range(16):
                    if first and k in (2, 3):
                        tb = k - 2
                        fn(proj[:, tb, 2 * WIDTH:2 * WIDTH + D], xin[:, tb, :], ACT.Square, accum_out=ssq_x[:, tb:tb + 1]).then_inc(x_ssq, 1)
                    if first and k == 7:
                        act.wait_ge(x_rstd, 1)
                        act.wait_ge(x_ssq, 2)
                    if k == 7 or k == 15:
                        c, acc_x, free = ((0, acc_a, a_free), (1, acc_b, b_free))[k // 8]
                        act.wait_ge(slot_used, S_PROJ + k + 1 + 16 * i)
                        fn(proj[:, 0, bass.ds(i * WIDTH + c * NCOL, NCOL)], acc_x[:, 0, :], ACT.Copy, scale=rstd_x[:, 0:1])
                        fn(proj[:, 1, bass.ds(i * WIDTH + c * NCOL, NCOL)], acc_x[:, 1, :], ACT.Copy, scale=rstd_x[:, 1:2]).then_inc(free, 1)
                    if k >= 4 or not first:
                        hi(S_PROJ + 4 + k, i, 16, 320 if last and k >= 12 else SLOT)

            pair(0, first=True)
            with act.Fori(1, N_PAIRS - 1) as i:
                pair(i)
            pair(N_PAIRS - 1, last=True)
            for k in range(RING):
                hi(S_ZC + k)

            for c in range(2):
                for tb in range(TB):
                    if 2 * c + tb:
                        act.wait_ge(c_ssq, 2 * c + tb)
                    fn(xin[:, 1, 1536:2048], c_tok[:, tb, c * LORA:(c + 1) * LORA], ACT.Square,
                       accum_out=ssq_c[:, 2 * c + tb:2 * c + tb + 1]).then_inc(c_ssq, 1)

            def small_evac(a):
                bank = aux[a % 4]
                if A_CT <= a < A_LG:
                    task_wait(act, a)
                    for n in range(2):
                        kt = 2 * (a - A_CT) + n
                        fn(cT_hi[:, kt, :], bank[:, n * SEQ:(n + 1) * SEQ], ACT.Copy,
                           scale=(g_q if kt < 4 else g_kv)[:, kt % 4:kt % 4 + 1]).then_inc(cT_hi_done, 1)
                elif A_BAND <= a < A_PW:
                    task_wait(act, a)
                    g = a - A_BAND
                    fn(y1_hi[:, 2 * g:2 * g + 2, :].rearrange("p n t -> p (n t)"), bank[:, :], ACT.Copy).then_inc(mT_hi_done, 1)
                elif A_YB <= a < A_QK:
                    task_wait(act, a)
                    for n in range(2):
                        f = 2 * (a - A_YB) + n
                        fn(y0_hi[:, f, :], bank[:, n * SEQ:(n + 1) * SEQ], ACT.Copy, scale=g_pool[:, f:f + 1]).then_inc(yb_hi_done, 1)
                elif a >= A_QK:
                    task_wait(act, a)
                    n0 = 2 * (a - A_QK)
                    dst = (qT_all if n0 < 4 else kT_all)[:, n0 % 4:n0 % 4 + 2, :].rearrange("p h t -> p (h t)")
                    fn(dst, bank[:, :], ACT.Copy).then_inc(aux_free[a % 4], 1)
                    if a == A_QK + 3:
                        act.dma_start(swap, consts[:, K_SWAP:K_BAND]).then_inc(swap_landed, 16)

            z = 0
            for k, kind in enumerate(ZC_SLOTS):
                for a in ZC_TASKS.get(k, ()):
                    small_evac(a)
                if k == 1:
                    fn(zb, zb, ACT.Silu).then_inc(z_silu, 1)
                    act.wait_ge(angle_done, 1)
                    fn(rope_tab[:, :], rope_tab[:, :], ACT.Sin).then_inc(table_done, 1)
                if k == 3:
                    fn(za, za, ACT.Silu).then_inc(z_silu, 1)
                if kind == "z":
                    z += 1
                    if z % 8 == 0:
                        c, acc_x, free = ((0, acc_b, b_free), (1, acc_a, a_free))[z // 8 - 1]
                        act.wait_ge(slot_used, S_ZC + k + 1)
                        task_wait(act, A_LG - 1)
                        for tb in range(TB):
                            ins = fn(zc[:, tb, c * NCOL:(c + 1) * NCOL], acc_x[:, tb, :], ACT.Silu, scale=rstd_x[:, tb:tb + 1])
                        ins.then_inc(free, 1)
                nxt = S_ZC + k + RING
                hi(nxt, n=SLOT if k + RING >= len(ZC_SLOTS) or ZC_SLOTS[k + RING] == "z" else 512)
            act.wait_ge(soft_arg, 1)
            fn(soft, soft, ACT.Exp).then_inc(soft_exp, 1)
            act.wait_ge(soft_exp, 1)
            fn(soft, soft, ACT.Ln, bias=1.0).then_inc(soft_done, 1)

            def tanh_gate(n):
                act.wait_ge(bias_added, 2 * n + 2)
                fn(gate, gate, ACT.Tanh, scale=0.5).then_inc(gate_done, 1)

            scale = float(NOPE + ROPE) ** -0.5
            with act.Fori(0, 4) as i:
                for k in range(16):
                    j = k % 2
                    if k in (4, 5, 6, 7):
                        bank = aux[(A_B0 + k - 4) % 4]
                        task_wait(act, A_B0 + k - 4, i)
                    if k == 4:
                        fn(q_raw, bank[:, 0:SEQ], ACT.Copy).then_inc(q_raw_done, 1)
                    for n in range(2):
                        if k == 5:
                            fn(qn[n], bank[:, n * SEQ:(n + 1) * SEQ], ACT.Copy).then_inc(qn_done, 1)
                        if k == 6:
                            fn(kn[n], bank[:, n * SEQ:(n + 1) * SEQ], ACT.Copy).then_inc(kv_done, 1)
                        if k == 7:
                            fn(vh[n], bank[:, :].rearrange("p (b h d) -> p b h d", b=TB, h=2)[:, :, n, :], ACT.Copy).then_inc(kv_done, 1)
                    if k in (8, 9):
                        act.wait_ge(m_done, 2 * i + j + 1)
                        for tb, lo, hi_ in ((0, 0, 128), (1, 128, 384)):
                            fn(sc[j][:, lo:hi_], sc[j][:, lo:hi_], ACT.Exp, bias=neg_m[j][:, tb:tb + 1], scale=scale,
                               accum_out=row_sum[j][:, tb:tb + 1]).then_inc(p_done, 1)
                    if k in (10, 11):
                        bank = aux[(A_B0 + 6 + j) % 4]
                        task_wait(act, A_B0 + 6 + j, i)
                        fn(pT[j].rearrange("p n q -> p (n q)"), bank[:, 0:384], ACT.Copy).then_inc(pT_done, 1)
                    if k == 11:
                        tanh_gate(i)
                    if k in (14, 15):
                        task_wait(act, A_B0 + 10 + j, i)
                        fn(y1_hi[:, bass.ds(2 * i + j, 1), :].rearrange("p n t -> p (n t)"), aux[(A_B0 + 10 + j) % 4][:, 0:SEQ], ACT.Copy).then_inc(ya_hi_done, 1)
                    if k < 4:
                        act.wait_ge(second_landed[k], 16 * i + 16)
                    hi(S_B0 + k + RING, i, 16, 8 * ROPE if k == 0 else SLOT)

            with act.Fori(0, 4) as i:
                for k in range(12):
                    if k == 0:
                        act.wait_ge(b_last_done, i + 1)
                        head = bcum[:, bass.ds(i, 1), :].rearrange("p h t -> p (h t)")
                        fn(g_q_dec, head, ACT.Exp, scale=1.0 / G_TAU).then_inc(decays, 1)
                        fn(g_k_dec, head, ACT.Exp, scale=-1.0 / G_TAU).then_inc(decays, 1)
                        for c in range(4):
                            cols = slice(c * CHUNK, (c + 1) * CHUNK)
                            ins = fn(g_k_end[:, cols], bcum[:, bass.ds(i, 1), cols].rearrange("p h t -> p (h t)"), ACT.Exp,
                                     scale=-1.0 / G_TAU, bias=b_last[:, c:c + 1])
                        ins.then_inc(decays, 1)
                        fn(decay, b_last, ACT.Exp).then_inc(decays, 1)
                        fn(g_v, v_tok[:, :, bass.ds(i * G_DV, G_DV)], ACT.Copy).then_inc(g_v_done, 1)
                    if k == 6:
                        for tb in range(TB):
                            task_wait(act, A_B1 + 4 + tb, i)
                            if tb:
                                act.wait_ge(o_ssq, 2 * i + 1)
                            fn(g_junk, aux[(A_B1 + 4 + tb) % 4][:, 0:G_DV], ACT.Square, accum_out=ssq_o[:, tb:tb + 1]).then_inc(o_ssq, 1)
                    if k == 7:
                        tanh_gate(4 + i)
                    if k == 9:
                        for n in range(2):
                            task_wait(act, A_B1 + 6 + n, i)
                            fn(y0_hi[:, bass.ds(2 * i + n, 1), :].rearrange("p n t -> p (n t)"), aux[(A_B1 + 6 + n) % 4][:, 0:SEQ], ACT.Copy,
                               scale=g_gla[:, bass.ds(2 * i + n, 1)]).then_inc(yc_hi_done, 1)
                    hi(S_B1 + k + RING, i, 12)

            def merged_hi(n):
                task_wait(act, A_MT + n)
                if n == 0:
                    act.wait_ge(slot_used, S_B2 + 36 + 8)
                fn(xT_hi[:, 2 * n:2 * n + 2, :].rearrange("p n t -> p (n t)"), aux[n % 4][:, :], ACT.Copy, scale=0.5).then_inc(mg_hi_done, 1)

            with act.Fori(0, 3) as i:
                for k in range(12):
                    if k == 7:
                        tanh_gate(8 + i)
                    hi(S_B2 + k + RING, i, 12)
            for k in range(12):
                if k == 7:
                    tanh_gate(11)
                if 8 <= k <= 10:
                    merged_hi(2 * (k - 8))
                    merged_hi(2 * (k - 8) + 1)
                hi(S_B2 + 36 + k + RING)

            def squares(c, tb):
                fn(proj[:, 1, R_V:R_V + NCOL], x_res[:, tb, c * NCOL:(c + 1) * NCOL], ACT.Square,
                   accum_out=ssq_f[:, 4 * tb + c:4 * tb + c + 1]).then_inc(f_ssq, 1)

            for k in range(32):
                if k in (3, 4):
                    merged_hi(k + 3)
                if k in (8, 16, 24):
                    c = k // 8 - 1
                    act.wait_ge(res_done, 2 * c + 2)
                    for tb in range(TB):
                        if 2 * c + tb:
                            act.wait_ge(f_ssq, 2 * c + tb)
                        squares(c, tb)
                if S_OUT + k + RING < S_END:
                    hi(S_OUT + k + RING)
            for tb in range(TB):
                act.wait_ge(f_ssq, 6 + tb)
                act.wait_ge(res_done, 7 + tb)
                squares(3, tb)
                act.wait_ge(f_rstd, tb + 1)
                act.wait_ge(y_done, 7 + tb)
                fn(y_out[:, tb, WIDTH:], y_out[:, tb, WIDTH:], ACT.Copy, scale=rstd_f[:, tb:tb + 1]).then_inc(f_done_act, 1)

        @block.vector
        def _(dve):
            v = nc.vector

            def lo(s, i=0, per=0, n=SLOT):
                k = s % RING
                dve.wait_ge(hi_ready, s + 1 + per * i)
                v.tensor_tensor(w_lo[:, k, 0:n], raw[:, k, 0:n], w_hi[:, k, 0:n].bitcast(F32), ALU.subtract).then_inc(lo_ready, 1)

            def lo_of(dst, bank, scale_, hi_):
                return v.scalar_tensor_tensor(out=dst, in0=bank, scalar=scale_, in1=hi_.bitcast(F32), op0=ALU.mult, op1=ALU.subtract)

            dve.wait_ge(gains_turned, 1)
            v.tensor_copy(gains[:, 0:16], acc_a[:, 0, 0:16]).then_inc(gains_done, 1)
            dve.wait_ge(gains_done, 1)
            v.memset(stat[:, 60:61], 0.0).then_inc(a_free, 1)
            for kt in range(KT):
                dve.wait_ge(xT_hi_done, kt // 2 * 2 + 2)
                ins = lo_of(xT_lo[:, kt, :], aux[(kt // 2) % 4][:, (kt % 2) * SEQ:(kt % 2 + 1) * SEQ], g_norm[:, kt:kt + 1], xT_hi[:, kt, :])
                ins.then_inc(xT_lo_done, 1)
                if kt % 2 == 1:
                    dve.wait_ge(xT_lo_done, kt + 1)
                    dve.sem_inc(aux_free[(kt // 2) % 4], 1)
                if kt % 2 == 1:
                    lo(S_PROJ + kt // 2)

            def pair(i, first=False, last=False):
                for k in range(4 if first else 0, 16):
                    if first and k == 6:
                        dve.wait_ge(gains_turned, 2)
                        v.tensor_copy(gains[:, 16:44], acc_b[:, 0, 0:28]).then_inc(gains_done, 1)
                        dve.wait_ge(gains_done, 2)
                        v.memset(stat[:, 61:62], 0.0).then_inc(b_free, 1)
                    lo(S_PROJ + 4 + k, i, 16, 320 if last and k >= 12 else SLOT)

            pair(0, first=True)
            with dve.Fori(1, N_PAIRS - 1) as i:
                pair(i)
            v.memset(ones, 1.0).then_inc(diag_done, 1)
            dve.wait_ge(x_rstd, 1)
            for tb in range(TB):
                v.tensor_scalar(rstd_diag[:, tb, :], ident, rstd_x[:, tb:tb + 1], None, ALU.mult).then_inc(diag_done, 1)
            pair(N_PAIRS - 1, last=True)
            for k in range(RING):
                lo(S_ZC + k)
            bank = aux[A_SMALL % 4]
            task_wait(dve, A_SMALL)
            v.tensor_copy(rstd_row, bank[0:ROPE + G_RANK, SEQ:2 * SEQ]).then_inc(row_done, 1)
            dve.wait_ge(row_done, 1)
            v.tensor_tensor(kr_raw, bank[0:ROPE, 0:SEQ], rstd_row[0:ROPE, :], ALU.mult).then_inc(kr_done, 1)
            v.tensor_tensor(gateT, bank[ROPE:ROPE + G_RANK, 0:SEQ], rstd_row[ROPE:ROPE + G_RANK, :], ALU.mult).then_inc(gateT_done, 1)
            dve.wait_ge(kr_done, 1)
            dve.wait_ge(gateT_done, 1)
            dve.sem_inc(aux_free[A_SMALL % 4], 1)
            dve.wait_ge(c_rstd, 1)
            for c in range(2):
                for tb in range(TB):
                    part_ = c_tok[:, tb, c * LORA:(c + 1) * LORA]
                    v.tensor_scalar(part_, part_, rstd_c[:, 2 * c + tb:2 * c + tb + 1], None, ALU.mult).then_inc(c_scaled, 1)

            def small_evac(a):
                bank = aux[a % 4]
                task_wait(dve, a)
                if a == A_KR:
                    dve.wait_ge(table_done, 1)
                    v.tensor_tensor(krT, kr_raw, cos_tab[0:ROPE, :], ALU.mult).then_inc(krT_part, 1)
                    v.tensor_tensor(q_raw[0:ROPE, :], bank[0:ROPE, 0:SEQ], sin_tab[0:ROPE, :], ALU.mult).then_inc(krT_part, 1)
                    dve.wait_ge(krT_part, 2)
                    dve.sem_inc(aux_free[a % 4], 1)
                    v.tensor_tensor(krT, krT, q_raw[0:ROPE, :], ALU.add).then_inc(krT_done, 1)
                elif a < A_LG:
                    for n in range(2):
                        kt = 2 * (a - A_CT) + n
                        dve.wait_ge(cT_hi_done, 2 * (a - A_CT) + 2)
                        lo_of(cT_lo[:, kt, :], bank[:, n * SEQ:(n + 1) * SEQ], (g_q if kt < 4 else g_kv)[:, kt % 4:kt % 4 + 1],
                              cT_hi[:, kt, :]).then_inc(cT_lo_done, 1)
                    dve.wait_ge(cT_lo_done, kt + 1)
                    dve.sem_inc(aux_free[a % 4], 1)
                elif a < A_BAND:
                    for n in range(2):
                        h = 2 * (a - A_LG) + n
                        v.tensor_scalar(logit[:, h, :], bank[:, n * SEQ:(n + 1) * SEQ], b_gate[:, h:h + 1], None, ALU.add).then_inc(logit_done, 1)
                    dve.wait_ge(logit_done, h + 1)
                    dve.sem_inc(aux_free[a % 4], 1)
                    if a == A_BAND - 1:
                        v.scalar_tensor_tensor(out=soft, in0=logit, scalar=-1.0, in1=logit, op0=ALU.mult, op1=ALU.min).then_inc(soft_arg, 1)
                elif a < A_PW:
                    g = a - A_BAND
                    dve.wait_ge(mT_hi_done, g + 1)
                    v.tensor_tensor(y1_lo[:, 2 * g:2 * g + 2, :].rearrange("p n t -> p (n t)"), bank[:, :],
                                    y1_hi[:, 2 * g:2 * g + 2, :].rearrange("p n t -> p (n t)").bitcast(F32), ALU.subtract).then_inc(mT_lo_done, 1)
                    dve.wait_ge(mT_lo_done, g + 1)
                    dve.sem_inc(aux_free[a % 4], 1)
                elif a < A_YB:
                    g = a - A_PW
                    dve.wait_ge(z_silu, 1)
                    part_ = zb[:, :, g * 256:(g + 1) * 256]
                    v.tensor_tensor(part_, bank[:, :].rearrange("p (b n) -> p b n", b=TB), part_, ALU.mult).then_inc(yb_done, 1)
                    dve.wait_ge(yb_done, g + 1)
                    dve.sem_inc(aux_free[a % 4], 1)
                elif a < A_QK:
                    for n in range(2):
                        f = 2 * (a - A_YB) + n
                        dve.wait_ge(yb_hi_done, 2 * (a - A_YB) + 2)
                        lo_of(y0_lo[:, f, :], bank[:, n * SEQ:(n + 1) * SEQ], g_pool[:, f:f + 1], y0_hi[:, f, :]).then_inc(yb_lo_done, 1)
                    dve.wait_ge(yb_lo_done, f + 1)
                    dve.sem_inc(aux_free[a % 4], 1)

            for k, kind in enumerate(ZC_SLOTS):
                if k == 2:
                    small_evac(A_KR)
                for a in ZC_TASKS.get(k, ()):
                    if a != A_KR and a < A_QK:
                        small_evac(a)
                lo(S_ZC + k + RING, n=SLOT if k + RING >= len(ZC_SLOTS) or ZC_SLOTS[k + RING] == "z" else 512)
            v.memset(scan_keep, 1.0).then_inc(keep_set, 1)
            dve.wait_ge(keep_set, 1)
            v.memset(scan_keep.rearrange("p (c t) -> p c t", t=CHUNK)[:, :, 0:1], 0.0).then_inc(keep_set, 1)
            dve.wait_ge(soft_done, 1)
            v.scalar_tensor_tensor(out=logit, in0=logit, scalar=0.0, in1=soft, op0=ALU.min, op1=ALU.subtract).then_inc(log_a_done, 1)
            dve.wait_ge(log_a_done, 1)
            dve.wait_ge(keep_set, 2)
            task_wait(dve, A_QK - 1)
            v.tensor_tensor_scan(bcum.rearrange("p h t -> p (h t)"), scan_keep, logit.rearrange("p h t -> p (h t)"), 0.0, ALU.mult, ALU.add).then_inc(bcum_done, 1)

            def bias(n, used):
                dve.wait_ge(slot_used, used)
                dve.wait_ge(bias_landed, 16 * n + 16)
                for tb in range(TB):
                    v.scalar_tensor_tensor(out=gate[:, tb, :], in0=acc_b[:, tb, :], scalar=rstd_x[:, tb:tb + 1], in1=bias_row,
                                           op0=ALU.mult, op1=ALU.add).then_inc(bias_added, 1)
                dve.wait_ge(bias_added, 2 * n + 2)
                dve.sem_inc(b_free, 1)

            def merge(n, i, first, used):
                cols = bass.ds(i * NCOL, NCOL)
                dve.wait_ge(slot_used, used)
                dve.wait_ge(gate_done, n + 1)
                dst = merged[:, :, cols] if first else gate
                v.scalar_tensor_tensor(out=dst, in0=gate, scalar=1.0, in1=acc_a, op0=ALU.add, op1=ALU.mult).then_inc(gated, 1)
                dve.wait_ge(gated, n + 1)
                dve.sem_inc(a_free, 1)
                if first:
                    dve.sem_inc(merged_done, 1)
                else:
                    v.tensor_tensor(merged[:, :, cols], merged[:, :, cols], gate, ALU.add).then_inc(merged_done, 1)

            with dve.Fori(0, 4) as i:
                for k in range(16):
                    j = k % 2
                    if k == 4:
                        dve.wait_ge(q_raw_done, i + 1)
                        v.tensor_tensor(rope_tmp, q_raw, cos_tab, ALU.mult).then_inc(rope_part, 1)
                    if k == 5:
                        dve.wait_ge(rope_part, 2 * i + 1)
                        dve.wait_ge(swapped, i + 1)
                        v.tensor_tensor(q_raw, aux[A_B0 % 4][:, SEQ:2 * SEQ], sin_tab, ALU.mult).then_inc(rope_part, 1)
                        dve.wait_ge(rope_part, 2 * i + 2)
                        dve.sem_inc(aux_free[A_B0 % 4], 1)
                        for n in range(2):
                            rows_ = slice(n * ROPE, (n + 1) * ROPE)
                            v.tensor_tensor(qr[n], rope_tmp[rows_, :], q_raw[rows_, :], ALU.add).then_inc(qr_done, 1)
                        dve.wait_ge(qn_done, 2 * i + 2)
                        dve.sem_inc(aux_free[(A_B0 + 1) % 4], 1)
                    if k in (6, 7):
                        dve.wait_ge(kv_done, 4 * i + 2 * (k - 5))
                        dve.sem_inc(aux_free[(A_B0 + k - 4) % 4], 1)
                    if k in (8, 9):
                        bank = aux[(A_B0 + 4 + j) % 4]
                        dve.wait_ge(rest_landed, 16)
                        task_wait(dve, A_B0 + 4 + j, i)
                        apart(dve)
                        for tb, lo_, hi_ in ((0, 0, 128), (1, 128, 384)):
                            v.tensor_tensor_reduce(sc[j][:, lo_:hi_], bank[:, lo_:hi_], mask[:, SEQ - (hi_ - lo_):SEQ], 1.0, NEG * 2,
                                                   ALU.add, ALU.max, mx[j][:, tb:tb + 1]).then_inc(s_done, 1)
                        dve.wait_ge(s_done, 2 * (2 * i + j + 1))
                        dve.sem_inc(aux_free[(A_B0 + 4 + j) % 4], 1)
                        v.tensor_scalar(neg_m[j], mx[j], -(float(NOPE + ROPE) ** -0.5), None, ALU.mult).then_inc(m_done, 1)
                    if k in (10, 11):
                        dve.wait_ge(p_done, 2 * (2 * i + j + 1))
                        v.reciprocal(row_inv[j], row_sum[j]).then_inc(inv_done, 1)
                        dve.wait_ge(pT_done, 2 * i + j + 1)
                        dve.sem_inc(aux_free[(A_B0 + 6 + j) % 4], 1)
                    if k == 11:
                        bias(i, S_B0 + 12 + 16 * i)
                    if k in (12, 13):
                        bank = aux[(A_B0 + 8 + j) % 4]
                        task_wait(dve, A_B0 + 8 + j, i)
                        dve.wait_ge(inv_done, 2 * i + j + 1)
                        dve.wait_ge(z_silu, 2)
                        for tb in range(TB):
                            v.scalar_tensor_tensor(out=yh[:, tb, j * P:(j + 1) * P], in0=bank[:, tb * P:(tb + 1) * P], scalar=row_inv[j][:, tb:tb + 1],
                                                   in1=za[:, tb, bass.ds(i * 2 * DV + j * DV, DV)], op0=ALU.mult, op1=ALU.mult).then_inc(ya_done, 1)
                        dve.wait_ge(ya_done, 2 * (2 * i + j + 1))
                        dve.sem_inc(aux_free[(A_B0 + 8 + j) % 4], 1)
                    if k in (14, 15):
                        dve.wait_ge(ya_hi_done, 2 * i + j + 1)
                        cols = bass.ds(2 * i + j, 1)
                        v.tensor_tensor(y1_lo[:, cols, :].rearrange("p n t -> p (n t)"), aux[(A_B0 + 10 + j) % 4][:, 0:SEQ],
                                        y1_hi[:, cols, :].rearrange("p n t -> p (n t)").bitcast(F32), ALU.subtract).then_inc(ya_lo_done, 1)
                        dve.wait_ge(ya_lo_done, 2 * i + j + 1)
                        dve.sem_inc(aux_free[(A_B0 + 10 + j) % 4], 1)
                    if k == 15:
                        merge(i, i, True, S_B0 + 16 + 16 * i)
                    lo(S_B0 + k + RING, i, 16, 8 * ROPE if k == 0 else SLOT)

            task_wait(dve, A_B0 + 11, 3)
            v.memset(g_att[0:CHUNK, :, CHUNK:P], 0.0).then_inc(att_zero, 1)
            v.memset(g_att[CHUNK:P, :, 0:CHUNK], 0.0).then_inc(att_zero, 1)
            with dve.Fori(0, 4) as i:
                for k in range(12):
                    if k == 0:
                        head = bcum[:, bass.ds(i, 1), :].rearrange("p h (c t) -> p (h c) t", t=CHUNK)
                        v.tensor_scalar(b_last, head[:, :, CHUNK - 1], 1.0 / G_TAU, None, ALU.mult).then_inc(b_last_done, 1)
                        qh, kh = (m[:, bass.ds(i, 1), :].rearrange("p h t -> p (h t)") for m in (qT_all, kT_all))
                        dve.wait_ge(decays, 4 * i + 1)
                        v.scalar_tensor_tensor(out=g_q_dec, in0=qh, scalar=float(G_DK) ** -0.5, in1=g_q_dec, op0=ALU.mult, op1=ALU.mult).then_inc(g_dec_done, 1)
                        dve.wait_ge(decays, 4 * i + 2)
                        v.tensor_tensor(g_k_dec, kh, g_k_dec, ALU.mult).then_inc(g_dec_done, 1)
                        dve.wait_ge(decays, 4 * i + 3)
                        v.tensor_tensor(g_k_end, kh, g_k_end, ALU.mult).then_inc(g_dec_done, 1)
                    if k == 2:
                        bank = aux[A_B1 % 4]
                        task_wait(dve, A_B1, i)
                        for r in range(2):
                            rows_ = slice(r * CHUNK, (r + 1) * CHUNK)
                            v.tensor_copy(g_att[rows_, :, rows_], bank[rows_, 0:SEQ].rearrange("p (b i) -> p b i", b=TB)[:, :, rows_]).then_inc(att_copied, 1)
                        dve.wait_ge(att_copied, 2 * i + 2)
                        dve.sem_inc(aux_free[A_B1 % 4], 1)
                    if k == 3:
                        task_wait(dve, A_B1 + 1, i)
                        v.tensor_copy(g_k_tok, aux[(A_B1 + 1) % 4][:, 0:SEQ].rearrange("p (b d) -> p b d", b=TB)).then_inc(k_tok_done, 1)
                        dve.wait_ge(k_tok_done, i + 1)
                        dve.sem_inc(aux_free[(A_B1 + 1) % 4], 1)
                    if k == 4:
                        task_wait(dve, A_B1 + 2, i)
                        dve.wait_ge(decays, 4 * i + 4)
                        b2, b3 = aux[(A_B1 + 2) % 4], aux[(A_B1 + 3) % 4]
                        v.tensor_copy(g_state[:, 0, :], b2[:, 0:G_DV]).then_inc(state_step, 1)
                        dve.wait_ge(state_step, 3 * i + 1)
                        task_wait(dve, A_B1 + 3, i)
                        v.scalar_tensor_tensor(out=g_state[:, 1, :], in0=g_state[:, 0, :], scalar=decay[:, 1:2], in1=b3[:, 0:G_DV],
                                               op0=ALU.mult, op1=ALU.add).then_inc(state_step, 1)
                        dve.wait_ge(state_step, 3 * i + 2)
                        dve.sem_inc(aux_free[(A_B1 + 3) % 4], 1)
                        v.scalar_tensor_tensor(out=g_state[:, 2, :], in0=g_state[:, 1, :], scalar=decay[:, 2:3], in1=b2[:, G_DV:2 * G_DV],
                                               op0=ALU.mult, op1=ALU.add).then_inc(state_step, 1)
                        dve.wait_ge(state_step, 3 * i + 3)
                        dve.sem_inc(aux_free[(A_B1 + 2) % 4], 1)
                    if k == 7:
                        bias(4 + i, S_B1 + 8 + 12 * i)
                        dve.wait_ge(o_rstd, i + 1)
                        for tb in range(TB):
                            v.scalar_tensor_tensor(out=yh[:, tb, :], in0=aux[(A_B1 + 4 + tb) % 4][:, 0:G_DV], scalar=rstd_o[:, tb:tb + 1],
                                                   in1=zc[:, tb, bass.ds(i * G_DV, G_DV)], op0=ALU.mult, op1=ALU.mult).then_inc(yc_done, 1)
                        dve.wait_ge(yc_done, 2 * i + 2)
                        dve.sem_inc(aux_free[(A_B1 + 4) % 4], 1)
                        dve.sem_inc(aux_free[(A_B1 + 5) % 4], 1)
                    if k == 9:
                        for n in range(2):
                            cols = bass.ds(2 * i + n, 1)
                            dve.wait_ge(yc_hi_done, 2 * i + n + 1)
                            lo_of(y0_lo[:, cols, :].rearrange("p n t -> p (n t)"), aux[(A_B1 + 6 + n) % 4][:, 0:SEQ], g_gla[:, cols],
                                  y0_hi[:, cols, :].rearrange("p n t -> p (n t)")).then_inc(yc_lo_done, 1)
                        dve.wait_ge(yc_lo_done, 2 * i + 2)
                        dve.sem_inc(aux_free[(A_B1 + 6) % 4], 1)
                        dve.sem_inc(aux_free[(A_B1 + 7) % 4], 1)
                    if k == 11:
                        merge(4 + i, i, False, S_B1 + 12 + 12 * i)
                    lo(S_B1 + k + RING, i, 12)

            def merged_lo(n):
                dve.wait_ge(mg_hi_done, n + 1)
                lo_of(xT_lo[:, 2 * n:2 * n + 2, :].rearrange("p n t -> p (n t)"), aux[n % 4][:, :], 0.5,
                      xT_hi[:, 2 * n:2 * n + 2, :].rearrange("p n t -> p (n t)")).then_inc(mg_lo_done, 1)
                dve.wait_ge(mg_lo_done, n + 1)
                dve.sem_inc(aux_free[n % 4], 1)

            with dve.Fori(0, 3) as i:
                for k in range(12):
                    if k == 7:
                        bias(8 + i, S_B2 + 8 + 12 * i)
                    if k == 11:
                        merge(8 + i, i, False, S_B2 + 12 + 12 * i)
                    lo(S_B2 + k + RING, i, 12)
            for k in range(12):
                if k == 7:
                    bias(11, S_B2 + 36 + 8)
                if 8 <= k <= 10:
                    merged_lo(2 * (k - 8))
                    merged_lo(2 * (k - 8) + 1)
                if k == 11:
                    merge(11, 3, False, S_B2 + 48)
                lo(S_B2 + 36 + k + RING)

            def residual(c, tb):
                cols = slice(c * NCOL, (c + 1) * NCOL)
                acc_x = (acc_b, acc_a)[c % 2]
                v.tensor_tensor(x_res[:, tb, cols], acc_x[:, tb, :], x_res[:, tb, cols], ALU.add).then_inc(res_done, 1)

            def gained(c, tb):
                cols = slice(c * NCOL, (c + 1) * NCOL)
                dve.wait_ge(res_done, 2 * c + tb + 1)
                v.tensor_tensor(y_out[:, tb, cols], x_res[:, tb, cols], fnorm_row[:, cols], ALU.mult).then_inc(y_done, 1)

            for k in range(32):
                if k in (3, 4):
                    merged_lo(k + 3)
                if k == 7:
                    dve.wait_ge(x_again, 16)
                if k in (7, 15, 23):
                    c = k // 8
                    dve.wait_ge(slot_used, S_OUT + k + 1)
                    for tb in range(TB):
                        residual(c, tb)
                    dve.wait_ge(res_done, 2 * c + 2)
                    dve.sem_inc((b_free, a_free)[c % 2], 1)
                if k in (9, 17, 25):
                    dve.wait_ge(mg_lo_done, 8)
                    dve.wait_ge(fnorm_landed, 16)
                    for tb in range(TB):
                        gained(k // 8 - 1, tb)
                if k == 26:
                    dve.wait_ge(f_ssq, 6)
                    v.tensor_reduce(ssq_ft, ssq_f.rearrange("p (b c) -> p b c", b=TB)[:, :, 0:3], AX_X, ALU.add).then_inc(f_sum, 1)
                    dve.wait_ge(f_sum, 1)
                    v.tensor_scalar(ssq_ft, ssq_ft, 1.0 / D, EPS, ALU.mult, ALU.add).then_inc(f_sum, 1)
                if S_OUT + k + RING < S_END:
                    lo(S_OUT + k + RING)
            for tb in range(TB):
                dve.wait_ge(last_done, tb + 1)
                residual(3, tb)
                gained(3, tb)
                dve.wait_ge(f_sum, 2)
                dve.wait_ge(f_ssq, 7 + tb)
                v.scalar_tensor_tensor(out=f_mean[:, tb:tb + 1], in0=ssq_f[:, 4 * tb + 3:4 * tb + 4], scalar=1.0 / D, in1=ssq_ft[:, tb:tb + 1],
                                       op0=ALU.mult, op1=ALU.add).then_inc(f_ms, 1)
                dve.wait_ge(f_rstd, tb + 1)
                v.tensor_scalar(y_out[:, tb, 0:WIDTH], y_out[:, tb, 0:WIDTH], rstd_f[:, tb:tb + 1], None, ALU.mult).then_inc(f_done, 1)


_INS = ["x", "positions", "norm_g", "w_in", "b_merge", "mla_q_norm", "mla_kv_norm", "mla_w_uq", "mla_w_ukv", "pool_w",
        "pool_scale", "gla_w_gate", "gla_b_gate", "gla_norm", "w_branch", "w_out", "final_norm"]


def kernel(**inputs):
    import concourse.bacc as _bacc
    from concourse.bass_utils import run_bass_kernel_spmd as _run

    nc = _bacc.Bacc("TRN2", target_bir_lowering=False, num_devices=1)
    arrays = {f"in_{name}_dram": np.ascontiguousarray(inputs[name]) for name in _INS}
    arrays["shape_constants_dram"] = shape_constants()
    args = [nc.dram_tensor(n, a.shape, mybir.dt.from_np(a.dtype), kind="ExternalInput").ap() for n, a in arrays.items()]
    out = nc.dram_tensor("out_dram", (1, SEQ, D), F32, kind="ExternalOutput").ap()
    trunk_kernel(nc, *args, out)
    r = _run(nc, [arrays], core_ids=[0])
    return r.results[0]["out_dram"]
```
